# Optimizing a Trainium2 kernel written in Bass

```python
import jax, jax.numpy as jnp
from jax import lax
import numpy as np

D_MODEL = 1024
BATCH = 1
SEQ = 512
DEPTH = 1

MEM_LEN = 256
CONV_WIDTH = 512
CONV_K = 3
HG_HEADS = 4
HG_F = 128
HG_I = 128
HG_QK = HG_HEADS * HG_F
HG_WIDTH = HG_HEADS * HG_I
HG_CHUNK = 32
MEM_HEADS = 4
MEM_HEAD_DIM = 128
MEM_WIDTH = MEM_HEADS * MEM_HEAD_DIM
N_BRANCH = 3
BRANCH_WIDTH = 512
D_FF = 4 * D_MODEL
ALPHA = (2.0 * DEPTH) ** 0.25
BETA = (8.0 * DEPTH) ** -0.25
LN_EPS = 1e-5
RMS_EPS = 1e-6
IN_SPLITS = (CONV_WIDTH, CONV_WIDTH, CONV_WIDTH, HG_QK, HG_QK, HG_WIDTH, HG_WIDTH, MEM_WIDTH, D_MODEL, D_MODEL, D_MODEL)
IN_COLS = sum(IN_SPLITS)

kernel_name = "hybrid_conv_hgrn2_memattn_postnorm"

def _layer_norm(x, g, b):
    xf = x.astype(jnp.float32)
    mu = jnp.mean(xf, axis=-1, keepdims=True)
    var = jnp.mean(jnp.square(xf - mu), axis=-1, keepdims=True)
    y = (xf - mu) * lax.rsqrt(var + LN_EPS) * g.astype(jnp.float32) + b.astype(jnp.float32)
    return y.astype(x.dtype)

def _short_conv_mixer(gate_b, gate_c, h, conv_w):
    u = gate_c * h
    seq = u.shape[1]
    u_pad = jnp.pad(u, ((0, 0), (CONV_K - 1, 0), (0, 0)))
    y = u_pad[:, 0:seq] * conv_w[0]
    for tap in range(1, CONV_K):
        y = y + u_pad[:, tap:tap + seq] * conv_w[tap]
    return gate_b * y

def _hgrn2_mixer(q, f_logit, i, g, lb, norm_w):
    bsz, seq, _ = q.shape
    n_chunk = seq // HG_CHUNK
    f32 = jnp.float32
    fl = f_logit.astype(f32)
    lb = lb.astype(f32)
    sig = jax.nn.sigmoid(fl)
    log_f = jnp.log(lb + (1.0 - lb) * sig)
    k = (1.0 - lb) * jax.nn.sigmoid(-fl)

    def to_chunks(t, d):
        return t.reshape(bsz, n_chunk, HG_CHUNK, HG_HEADS, d).transpose(0, 3, 1, 2, 4)

    qc = to_chunks(jax.nn.silu(q.astype(f32)), HG_F)
    kc = to_chunks(k, HG_F)
    vc = to_chunks(i.astype(f32), HG_I)
    bc = jnp.cumsum(to_chunks(log_f, HG_F), axis=3)
    b_ref = bc[:, :, :, HG_CHUNK // 2 - 1:HG_CHUNK // 2, :]
    b_last = bc[:, :, :, -1:, :]

    causal = jnp.tril(jnp.ones((HG_CHUNK, HG_CHUNK), dtype=bool))
    scores = jnp.einsum('bhntf,bhnsf->bhnts', qc * jnp.exp(bc - b_ref), kc * jnp.exp(b_ref - bc))
    scores = jnp.where(causal, scores, 0.0)
    o_intra = jnp.einsum('bhnts,bhnsv->bhntv', scores, vc)

    q_in = qc * jnp.exp(bc)
    k_out = kc * jnp.exp(b_last - bc)
    decay = jnp.exp(b_last[:, :, :, 0, :])

    def step(state, xs):
        q_n, k_n, v_n, dec_n = xs
        o_n = jnp.einsum('bhtf,bhfv->bhtv', q_n, state)
        state = dec_n[..., None] * state + jnp.einsum('bhsf,bhsv->bhfv', k_n, v_n)
        return state, o_n

    xs = (jnp.moveaxis(q_in, 2, 0), jnp.moveaxis(k_out, 2, 0), jnp.moveaxis(vc, 2, 0), jnp.moveaxis(decay, 2, 0))
    init = jnp.zeros((bsz, HG_HEADS, HG_F, HG_I), f32)
    _, o_inter = lax.scan(step, init, xs)
    o = o_intra + jnp.moveaxis(o_inter, 0, 2)

    o = o.transpose(0, 2, 3, 1, 4).reshape(bsz, seq, HG_HEADS, HG_I)
    o = o * lax.rsqrt(jnp.mean(o * o, axis=-1, keepdims=True) + RMS_EPS) * norm_w.astype(f32)
    o = o.reshape(bsz, seq, HG_WIDTH) * jax.nn.silu(g.astype(f32))
    return o.astype(q.dtype)

def _memory_attention(q, mem_k, mem_v):
    bsz, seq, _ = q.shape
    qh = q.reshape(bsz, seq, MEM_HEADS, MEM_HEAD_DIM)
    kh = mem_k.reshape(bsz, MEM_LEN, MEM_HEADS, MEM_HEAD_DIM)
    vh = mem_v.reshape(bsz, MEM_LEN, MEM_HEADS, MEM_HEAD_DIM)
    s = jnp.einsum('bthd,bmhd->bhtm', qh, kh).astype(jnp.float32) * (MEM_HEAD_DIM ** -0.5)
    p = jax.nn.softmax(s, axis=-1).astype(vh.dtype)
    o = jnp.einsum('bhtm,bmhd->bthd', p, vh)
    return o.reshape(bsz, seq, MEM_WIDTH)

def _hybrid_layer(x, mem, lb, w_in, conv_w, hg_norm_w, w_mem_k, w_mem_v, w_branch, b_gate, w_o,
                  ln1_g, ln1_b, w_up, w_down, ln2_g, ln2_b):
    bsz, seq, _ = x.shape
    proj = jnp.einsum('bsd,dc->bsc', x, w_in)
    split_idx = [int(v) for v in np.cumsum(IN_SPLITS)[:-1]]
    cb, cc, ch, hq, hf, hi, hg, mq, ga, gb, gc = jnp.split(proj, split_idx, axis=-1)

    y_a = _short_conv_mixer(cb, cc, ch, conv_w)
    y_b = _hgrn2_mixer(hq, hf, hi, hg, lb, hg_norm_w)
    y_c = _memory_attention(mq, jnp.einsum('bmd,dw->bmw', mem, w_mem_k), jnp.einsum('bmd,dw->bmw', mem, w_mem_v))

    b_ga, b_gb, b_gc = jnp.split(b_gate, N_BRANCH, axis=-1)
    merged = (jax.nn.sigmoid(ga + b_ga) * jnp.einsum('bsw,wd->bsd', y_a, w_branch[0])
              + jax.nn.sigmoid(gb + b_gb) * jnp.einsum('bsw,wd->bsd', y_b, w_branch[1])
              + jax.nn.sigmoid(gc + b_gc) * jnp.einsum('bsw,wd->bsd', y_c, w_branch[2]))
    mixed = jnp.einsum('bsd,de->bse', merged, w_o)
    x = _layer_norm(ALPHA * x + mixed, ln1_g, ln1_b)

    h = jnp.square(jax.nn.relu(jnp.einsum('bsd,df->bsf', x, w_up)))
    x = _layer_norm(ALPHA * x + jnp.einsum('bsf,fd->bsd', h, w_down), ln2_g, ln2_b)
    return x

def setup_inputs(seed: int = 0) -> dict:
    key = jax.random.key(seed)
    ks = jax.random.split(key, 20)
    nrm = jax.random.normal
    f32 = jnp.float32
    return {
        'x': nrm(ks[0], (BATCH, SEQ, D_MODEL), f32),
        'mem': nrm(ks[1], (BATCH, MEM_LEN, D_MODEL), f32),
        'lower_bounds': 0.02 * nrm(ks[2], (DEPTH, HG_QK), f32),
        'w_in': nrm(ks[3], (DEPTH, D_MODEL, IN_COLS), f32) * D_MODEL ** -0.5,
        'conv_w': nrm(ks[4], (DEPTH, CONV_K, CONV_WIDTH), f32) * CONV_K ** -0.5,
        'hg_norm_w': 1.0 + 0.02 * nrm(ks[5], (DEPTH, HG_I), f32),
        'w_mem_k': nrm(ks[6], (DEPTH, D_MODEL, MEM_WIDTH), f32) * D_MODEL ** -0.5,
        'w_mem_v': nrm(ks[7], (DEPTH, D_MODEL, MEM_WIDTH), f32) * (D_MODEL ** -0.5 * BETA),
        'w_branch': nrm(ks[8], (DEPTH, N_BRANCH, BRANCH_WIDTH, D_MODEL), f32) * (BRANCH_WIDTH ** -0.5 * BETA),
        'b_gate': 0.02 * nrm(ks[9], (DEPTH, N_BRANCH * D_MODEL), f32),
        'w_o': nrm(ks[10], (DEPTH, D_MODEL, D_MODEL), f32) * (D_MODEL ** -0.5 * BETA),
        'ln1_g': 1.0 + 0.02 * nrm(ks[11], (DEPTH, D_MODEL), f32),
        'ln1_b': 0.02 * nrm(ks[12], (DEPTH, D_MODEL), f32),
        'w_up': nrm(ks[13], (DEPTH, D_MODEL, D_FF), f32) * (D_MODEL ** -0.5 * BETA),
        'w_down': nrm(ks[14], (DEPTH, D_FF, D_MODEL), f32) * (D_FF ** -0.5 * BETA),
        'ln2_g': 1.0 + 0.02 * nrm(ks[15], (DEPTH, D_MODEL), f32),
        'ln2_b': 0.02 * nrm(ks[16], (DEPTH, D_MODEL), f32),
    }

def reference(x, mem, lower_bounds, w_in, conv_w, hg_norm_w, w_mem_k, w_mem_v, w_branch, b_gate, w_o,
              ln1_g, ln1_b, w_up, w_down, ln2_g, ln2_b):
    lb_soft = jax.nn.softmax(lower_bounds.astype(jnp.float32), axis=0)
    lb_all = jnp.cumsum(lb_soft, axis=0) - lb_soft[0:1]
    for layer in range(DEPTH):
        x = _hybrid_layer(x, mem, lb_all[layer], w_in[layer], conv_w[layer], hg_norm_w[layer],
                          w_mem_k[layer], w_mem_v[layer], w_branch[layer], b_gate[layer], w_o[layer],
                          ln1_g[layer], ln1_b[layer], w_up[layer], w_down[layer], ln2_g[layer], ln2_b[layer])
    return x


_drawn_inputs = setup_inputs


def setup_inputs(seed=0):
    import zlib

    import numpy as np

    out = dict(_drawn_inputs(seed))
    spreads = {}
    factors = {'mem': 6.068,
     'hg_norm_w': 64.0,
     'w_mem_k': 6.932,
     'w_mem_v': 5.81,
     'b_gate': 8.0,
     'ln1_g': 7.595,
     'ln1_b': 7.854,
     'ln2_g': 8.165,
     'ln2_b': 8.173}
    for name, (base, spread) in spreads.items():
        noise = np.random.default_rng([zlib.crc32(name.encode()), seed]).standard_normal(out[name].shape)
        drawn = base * np.exp(spread * noise) if base else spread * noise
        out[name] = __import__('jax').numpy.asarray(drawn.astype(out[name].dtype))
    for name, factor in factors.items():
        out[name] = (out[name] * factor).astype(out[name].dtype)
    return out
```

```python
from contextlib import ExitStack

import concourse.bass as bass
from concourse import mybir

F32 = mybir.dt.float32
F32R = mybir.dt.float32r
U32 = mybir.dt.uint32
ALU = mybir.AluOpType
ACT = mybir.ActivationFunctionType
AX_X = mybir.AxisListType.X

P = 128
T = 512
D = 1024
KD = D // P
M = 256
WID = 512
HEADS = WID // P
TB = T // P
C = 32
NCH = T // C
QD = P // C
DFF = 4 * D
DEPTH = 1
ALPHA = (2.0 * DEPTH) ** 0.25
LN_EPS = 1e-5
RMS_EPS = 1e-6
SCALE = float(P) ** -0.5
SLAB = 2048
MAIN = 4

COL = dict(cb=0, cc=WID, ch=2 * WID, q=3 * WID, f=4 * WID, v=5 * WID, g=6 * WID, mq=7 * WID, gate=8 * WID)
PROJ = ["mq", "f", "q", "v", "g", "cc", "ch", "cb"]

S_PROJ, N_PROJ = 4, len(PROJ)
S_GATE, N_GATE = S_PROJ + 2 * N_PROJ, 6
S_OUT = S_GATE + 3 * N_GATE
S_MLP, N_MLP = S_OUT + 4, 8
G_MLP = DFF // D
M_PROJ, M_GATE = 8, 8 + 2 * 16
M_OUT = M_GATE + 3 * 16
M_MLP = M_OUT + 8

AUX_PRO = [("t%d" % i, 4 + i % 4) for i in range(13)]
AUX_HALF = ([("as%d" % b, 4 + b) for b in range(4)] + [("pt%d" % b, 4 + b) for b in range(4)]
            + [("pv0", 4), ("pv1", 5), ("ko0", 6), ("ko1", 7), ("sc0", 4), ("sc1", 5)]
            + [("kv%d%d" % (b, h), 6 + h) for b in range(TB) for h in range(2)]
            + [("out0", 4), ("out1", 5), ("ms0", 6), ("ms1", 7)])
AUX_LN = [("x%d%d" % (b, j), 4 + 2 * (b % 2) + j) for b in range(TB) for j in range(2)]


def uses(bank, seq):
    return sum(1 for _, b in seq if b == bank)


class Aux:

    def __init__(self, seq, before):
        self.seq = seq
        self.index = {n: i for i, (n, _) in enumerate(seq)}
        self.bank = dict(seq)
        self.first = sum(len(s) * r for s, r in before)
        self.before = {b: sum(uses(b, s) * r for s, r in before) for b in range(4, 8)}

    def done(self, name, it=0):
        return it * len(self.seq) + (self.first + self.index[name] + 1)

    def earlier(self, name, it=0):
        b = self.bank[name]
        return it * uses(b, self.seq) + (self.before[b] + uses(b, self.seq[:self.index[name]]))

    def read(self, name, it=0):
        return self.earlier(name, it) + 1


PRO = Aux(AUX_PRO, [])
HALF = Aux(AUX_HALF, [(AUX_PRO, 1)])
LNT = Aux(AUX_LN, [(AUX_PRO, 1), (AUX_HALF, 2)])


def build(nc, x, mem, lower_bounds, w_in, conv_w, hg_norm_w, w_mem_k, w_mem_v, w_branch, b_gate, w_o,
          ln1_g, ln1_b, w_up, w_down, ln2_g, ln2_b, out):
    ds = bass.ds
    with ExitStack() as ctx:
        def sb(name, shape, dt=F32):
            return ctx.enter_context(nc.sbuf_tensor(name, shape, dt))

        def sem(name):
            return ctx.enter_context(nc.semaphore(name))

        raw = sb("raw", [P, 2, SLAB])
        w_hi = sb("w_hi", [P, 4, SLAB], F32R)
        w_lo = sb("w_lo", [P, 4, SLAB], F32R)
        x_hi = sb("x_hi", [P, KD, T], F32R)
        x_lo = sb("x_lo", [P, KD, T], F32R)
        y_hi = sb("y_hi", [P, 3 * HEADS, T], F32R)
        y_lo = sb("y_lo", [P, 3 * HEADS, T], F32R)
        memt_hi = y_hi[:, 8:12, :].rearrange("p a (b m) -> p (a b) m", m=M)
        memt_lo = y_lo[:, 8:12, :].rearrange("p a (b m) -> p (a b) m", m=M)

        two = sb("two", [P, 6, 1024])
        x_tok = two[:, 0:4, :]
        mem_tok = two[:, 4:6, :]
        resid = two[:, 0:4, :]
        tiles4 = two[:, 4:6, :].rearrange("p a (b t) -> p (a b) t", t=T)

        def heads2(n):
            return two[:, n, :].rearrange("p (h t) -> p h t", h=2)

        kk, qq, lf, bc, aa, ee = (heads2(n) for n in range(6))
        q_mem = ee
        silu_g = kk
        conv_u = bc
        conv_y = lf
        o_sq = aa
        o_rstd = ee
        o_norm = aa

        def chunks(buf):
            return buf.rearrange("p h (n c) -> p (h n) c", c=C)

        small = sb("small", [P, 9 * 1024])
        states = small[:, 0:2048].rearrange("p (h n v) -> p h n v", h=2, v=P)
        probs_t = small[:, 0:2048].rearrange("p (h m t) -> p h m t", h=2, m=2)
        v_diag = small[:, 2048:4096].rearrange("p (r h c v) -> p r h c v", r=2, h=2, c=QD)
        probs = small[:, 2048:4096].rearrange("p (b h m) -> p b h m", b=TB, h=2)
        v_tok = small[:, 4096:5120].rearrange("p (b h v) -> p b h v", b=TB, h=2)
        kout_t = small[:, 5120:6144].rearrange("p (h b f) -> p h b f", h=2, b=TB)
        par_rows = small[0:41, 5120:5248]
        mem_v_half = small[:, 5120:5632].rearrange("p (m w) -> p m w", m=2)
        sc_diag = small[:, 6144:7168].rearrange("p (h b t) -> p h b t", h=2, b=TB)
        mem_k = small[:, 7168:8192].rearrange("p (h m) -> p h m", h=HEADS)
        mem_v = small[:, 8192:9216].rearrange("p (b w) -> p b w", b=2)
        causal_f = small[:, 0:128].rearrange("p (b t) -> p b t", b=TB)
        merged = small[:, 0:4096].rearrange("p (k t) -> p k t", k=KD)
        ln_par = small[:, 4096:8192].rearrange("p (n d) -> p n d", n=4)

        ident = sb("ident", [P, P])
        ones = sb("ones", [P, P])
        scan_keep = sb("scan_keep", [P, T], mybir.dt.uint8)
        causal = sb("causal", [P, TB, C], U32)
        par = sb("par", [P, 41])
        CONV_W, LB, NORM_W = 24, 36, 40
        lbw = sb("lbw", [P, 6, HEADS])
        eps = sb("eps", [P, 2])
        smx = sb("smx", [P, 4, TB, 2])
        decay = sb("decay", [P, 2, NCH])
        stats = sb("stats", [P, 2, 6])
        mv = sb("mv", [P, 2])
        lnw = sb("lnw", [P, 2])

        bank = [ctx.enter_context(nc.psum_tensor("bank%d" % n, [P, T], F32))[:, :] for n in range(8)]

        small_landed = sem("small_landed")
        mem_landed = [sem("mem_landed0"), sem("mem_landed1")]
        front_landed = sem("front_landed")
        x_landed = sem("x_landed")
        slab_landed = [sem("slab_landed0"), sem("slab_landed1")]
        x_again = sem("x_again")
        ln_landed = sem("ln_landed")
        stored = sem("stored")
        slab_hi = sem("slab_hi")
        slab_lo = sem("slab_lo")
        tile_done = sem("tile_done")
        main_read = [sem("main_read%d" % n) for n in range(MAIN)]
        aux_done = sem("aux_done")
        aux_read = {b: sem("aux_read%d" % b) for b in range(4, 8)}
        names = """ident_ready consts_ready lb_diff lb_exp lb_ready transposed_hi negmax_ready probs_ready vhalf_ready
            logf_ready diffs_ready exps_ready sig_q operands attn_hi v_diag_ready out_block sig_g
            conv_hi sq_ready rstd_ready hgrn_ready hgrn_hi branch_split merge_done merged_hi
            merged_split var_ready std_ready x1_ready x1_hi resid_ready relu_ready h_hi
            h_split h_made y_ready dve_chain pool_chain state_step conv_tapped ln_step front_hi front_lo""".split()
        (ident_ready, consts_ready, lb_diff, lb_exp, lb_ready, transposed_hi, negmax_ready, probs_ready, vhalf_ready,
         logf_ready, diffs_ready, exps_ready, sig_q, operands, attn_hi, v_diag_ready, out_block, sig_g,
         conv_hi, sq_ready, rstd_ready, hgrn_ready, hgrn_hi, branch_split, merge_done, merged_hi,
         merged_split, var_ready, std_ready, x1_ready, x1_hi, resid_ready, relu_ready, h_hi,
         h_split, h_made, y_ready, dve_chain, pool_chain, state_step, conv_tapped, ln_step, front_hi, front_lo) = (sem(n) for n in names)

        def proj_round(half):
            return half * 4 + 2

        def gate_round(i):
            return i * 4 + 10

        OUT_ROUND = 22

        def mlp_round(g):
            return g * 4 + 24

        def main_of(eng, rnd, t):
            eng.wait_ge(tile_done, rnd * MAIN + (t + 1))
            return bank[t % MAIN]

        def main_copied(eng, rnd, t):
            eng.wait_ge(main_read[t % MAIN], rnd + (t // MAIN + 1))

        def aux_of(eng, phase, name, it=0):
            eng.wait_ge(aux_done, phase.done(name, it))
            return bank[phase.bank[name]]

        def aux_copied(eng, phase, name, it=0):
            eng.wait_ge(aux_read[phase.bank[name]], phase.read(name, it))

        block = ctx.enter_context(nc.Block())

        def rows(w):
            return w.rearrange("(k p) c -> p k c", p=P)

        win, wup, wdn, wout = rows(w_in[0]), rows(w_up[0]), rows(w_down[0]), rows(w_o[0])
        win_256 = w_in[0].rearrange("(k p) (n c) -> p k n c", p=P, c=256)
        wmk, wmv = rows(w_mem_k[0]), rows(w_mem_v[0])
        wbr = w_branch[0].rearrange("i (k p) c -> p (i k) c", p=P)
        out_t = out[0].rearrange("(b p) d -> b p d", p=P)
        x_t = x[0].rearrange("(b p) d -> p b d", p=P)

        @block.sync
        def _(sp):
            def load(s, r, src, k):
                if not isinstance(s, int) or s >= 2:
                    sp.wait_ge(slab_lo, s - 1)
                if len(src.shape) == 4:
                    src = src.rearrange("p k n c -> p k (n c)")
                sp.dma_start(raw[:, r, :].rearrange("p (k c) -> p k c", k=k), src).then_inc(slab_landed[r], 16)

            for e in range(2):
                part = slice(e * WID, (e + 1) * WID)
                sp.dma_start(mem_tok[:, :, part], mem[0].rearrange("(b p) d -> p b d", p=P)[:, :, part])\
                    .then_inc(mem_landed[e], 16)
            for part in (slice(0, KD // 2), slice(KD // 2, KD)):
                sp.dma_start(raw[:, 0, :].rearrange("p (k c) -> p k c", k=KD)[:, part], wmk[:, part, 0:256])\
                    .then_inc(front_landed if part.start == 0 else slab_landed[0], 16)
            load(1, 1, wmk[:, :, 256:512], KD)
            sp.dma_start(x_tok, x_t).then_inc(x_landed, 16)
            for to, rows_of in ((par_rows[0:24], b_gate[0].rearrange("(r p) -> r p", p=P)),
                                (par_rows[24:36], conv_w[0].rearrange("t (r p) -> (t r) p", p=P)),
                                (par_rows[36:40], lower_bounds[0].rearrange("(r p) -> r p", p=P)),
                                (par_rows[40:41], hg_norm_w)):
                sp.dma_start(to, rows_of).then_inc(small_landed, 16)
            load(2, 0, wmv[:, :, 0:256], KD)
            load(3, 1, wmv[:, :, 256:512], KD)
            with sp.Fori(0, 2) as half:
                for j, name in enumerate(PROJ):
                    n = half + COL[name] // 256
                    load(half * N_PROJ + (S_PROJ + j), j % 2, win_256[:, :, ds(n, 1), :], KD)
            with sp.Fori(0, 3) as i:
                for h in range(2):
                    for j in range(2):
                        load(i * N_GATE + (S_GATE + 3 * h + j), (3 * h + j) % 2,
                             win[:, :, ds(i * D + (COL["gate"] + h * WID + j * 256), 256)], KD)
                    load(i * N_GATE + (S_GATE + 3 * h + 2), (3 * h + 2) % 2,
                         wbr[:, ds(i * HEADS, HEADS), h * WID:(h + 1) * WID], HEADS)
            sp.wait_ge(branch_split, 8)
            sp.dma_start(resid, x_t).then_inc(x_again, 16)
            for n, v in enumerate((ln1_g, ln1_b, ln2_g, ln2_b)):
                sp.dma_start(ln_par[:, n, :], v.to_broadcast((P, D))).then_inc(ln_landed, 16)
            for e in range(2):
                for h in range(2):
                    load(S_OUT + 2 * e + h, h, wout[:, 4 * h:4 * h + 4, e * WID:(e + 1) * WID], 4)
            with sp.Fori(0, G_MLP) as g:
                for j in range(4):
                    load(g * N_MLP + (S_MLP + j), j % 2, wup[:, :, ds(g * D + j * 256, 256)], KD)
                for e in range(2):
                    for h in range(2):
                        load(g * N_MLP + (S_MLP + 4 + 2 * e + h), h,
                             wdn[:, ds(g * KD + 4 * h, 4), e * WID:(e + 1) * WID], 4)
            for b in range(TB):
                for e in range(2):
                    part = slice(e * WID, (e + 1) * WID)
                    sp.wait_ge(y_ready, 2 * b + (e + 1))
                    sp.dma_start(out_t[b][:, part], resid[:, b, part]).then_inc(stored, 16)
            sp.wait_ge(stored, 16 * 2 * TB)

        @block.gpsimd
        def _(pool):
            chain = [0]

            def after(ins):
                ins.then_inc(pool_chain, 1)
                chain[0] += 1
                pool.wait_ge(pool_chain, chain[0])

            after(pool.memset(ident[:], 0.0))
            pool.affine_select(out=ident[:], in_=ident[:], compare_op=ALU.not_equal, fill=1.0, base=0,
                               pattern=[[-1, P]], channel_multiplier=1).then_inc(ident_ready, 1)
            pool.memset(ones[:], 1.0)
            pool.memset(scan_keep[:], 1)
            pool.memset(eps[:, 0:1], LN_EPS)
            pool.memset(eps[:, 1:2], RMS_EPS)
            pool.memset(sc_diag, 0.0)
            after(pool.memset(causal_f, 0.0))
            pool.memset(scan_keep[:].rearrange("p (n c) -> p n c", c=C)[:, :, 0:1], 0)
            for q in range(QD):
                part = causal_f[q * C:(q + 1) * C]
                after(pool.affine_select(out=part, in_=part, compare_op=ALU.is_gt, fill=1.0, base=0,
                                         pattern=[[0, TB], [-1, C]], channel_multiplier=1))
            pool.tensor_copy(causal[:], causal_f).then_inc(consts_ready, 1)

            for half in range(2):
                pool.wait_ge(aux_done, HALF.done("as0", half))
                pool.tensor_copy(mem_v_half, mem_v[:, :, half * 256:(half + 1) * 256]).then_inc(vhalf_ready, 1)
                pool.wait_ge(aux_done, HALF.done("pt3", half))
                pool.wait_ge(vhalf_ready, half + 1)
                after(pool.memset(small[:, 2048:4096], 0.0))
                for t in (6, 7):
                    main_copied(pool, proj_round(half), t)
                for b in range(TB):
                    if b >= 2:
                        pool.wait_ge(aux_done, HALF.done("kv%d1" % (b - 2), half))
                    for q in range(QD):
                        part = slice(q * C, (q + 1) * C)
                        cp = pool.tensor_copy(v_diag[part, b % 2, :, q, :], v_tok[part, b, :, :])
                        if q < QD - 1:
                            after(cp)
                    cp.then_inc(v_diag_ready, 1)
                    pool.wait_ge(v_diag_ready, half * TB + b + 1)
            pool.wait_ge(branch_split, 8)
            pool.memset(merged, 0.0).then_inc(merge_done, 1)
            for b in range(TB):
                pool.wait_ge(aux_done, LNT.done("x%d1" % b))
                pool.tensor_scalar(resid[:, b, :], resid[:, b, :], ALPHA, 1.0, ALU.mult, ALU.mult)\
                    .then_inc(resid_ready, 1)

        @block.scalar
        def _(act):
            def hi(s, slot, tiles=None):
                r = slot_raw[0]
                if tiles is not None:
                    act.wait_ge(tile_done, tiles)
                act.wait_ge(slab_landed[r], s * 8 + (16 - 8 * r))
                act.activation(w_hi[:, slot, :], raw[:, r, :], ACT.Copy).then_inc(slab_hi, 1)
                slot_raw[0] = 1 - r

            slot_raw = [0]

            for j in range(4):
                if j == 3:
                    act.wait_ge(front_landed, 16)
                    act.activation(w_hi[:, 0, 0:SLAB // 2], raw[:, 0, 0:SLAB // 2], ACT.Copy).then_inc(front_hi, 1)
                src = aux_of(act, PRO, "t%d" % j).rearrange("p (k m) -> p k m", k=2)
                act.activation(memt_hi[:, 2 * j:2 * j + 2, :], src, ACT.Copy).then_inc(transposed_hi, 1)
            act.wait_ge(slab_landed[0], 16)
            act.activation(w_hi[:, 0, SLAB // 2:SLAB], raw[:, 0, SLAB // 2:SLAB], ACT.Copy).then_inc(slab_hi, 1)
            slot_raw[0] = 1
            hi(1, 1)
            def x_parts(ks):
                for k in ks:
                    act.activation(x_hi[:, k, :], aux_of(act, PRO, "t%d" % (4 + k)), ACT.Copy)\
                        .then_inc(transposed_hi, 1)

            hi(2, 2)
            for s in range(4):
                if s == 2:
                    x_parts(range(0, 4))
                    hi(3, 3)
                    x_parts(range(4, KD))
                    hi(4, 0, 2)
                elif s == 3:
                    hi(5, 1, 4)
                for c in range(2):
                    src = main_of(act, 0, 2 * s + c)[:, 0:M]
                    dst = mem_k[:, 2 * s + c, :] if s < 2 else mem_v[:, c, (s - 2) * 256:(s - 1) * 256]
                    act.activation(dst, src, ACT.Copy).then_inc(main_read[(2 * s + c) % MAIN], 1)
            act.wait_ge(lb_diff, 1)
            act.activation(lbw[:, 1, :], lbw[:, 0, :], ACT.Exp).then_inc(lb_exp, 1)

            with act.Fori(0, 2) as half:
                s0 = half * N_PROJ + S_PROJ
                rnd = proj_round(half)

                def hi_next(r):
                    hi(s0 + (r + 2), (r + 2) % 4, rnd * MAIN + (2 * r - 2))

                hi_next(0)
                act.wait_ge(slab_lo, s0 + 3)
                for h in range(2):
                    act.activation(q_mem[:, h, :], main_of(act, rnd, h), ACT.Copy).then_inc(main_read[h], 1)
                hi_next(1)
                for h in range(2):
                    t = main_of(act, rnd, 2 + h)
                    act.activation(lf[:, h, :], t, ACT.Sigmoid)
                    act.activation(kk[:, h, :], t, ACT.Sigmoid, scale=-1.0).then_inc(main_read[2 + h], 1)
                main_copied(act, rnd, 3)
                act.wait_ge(lb_ready, 1)
                for h in range(2):
                    act.activation(lf[:, h, :], lf[:, h, :], ACT.Ln, bias=lbw[:, 4, ds(half * 2 + h, 1)],
                                   scale=lbw[:, 5, ds(half * 2 + h, 1)]).then_inc(logf_ready, 1)
                for b in range(TB):
                    act.wait_ge(negmax_ready, half * TB + (b + 1))
                    for h in range(2):
                        ex = act.activation(probs[:, b, h, :], bank[4 + b][:, h * M:(h + 1) * M], ACT.Exp,
                                            bias=smx[:, 1, b, h:h + 1], scale=SCALE,
                                            accum_out=smx[:, 2, b, h:h + 1])
                    ex.then_inc(aux_read[4 + b], 1)
                hi_next(2)
                for h in range(2):
                    act.activation(qq[:, h, :], main_of(act, rnd, 4 + h), ACT.Sigmoid).then_inc(sig_q, 1)
                act.wait_ge(diffs_ready, half * 2 + 1)
                act.activation(ee, aa, ACT.Exp).then_inc(exps_ready, 1)
                act.activation(aa, aa, ACT.Exp, scale=-1.0).then_inc(exps_ready, 1)
                act.wait_ge(diffs_ready, half * 2 + 2)
                act.activation(bc, bc, ACT.Exp).then_inc(exps_ready, 1)
                act.activation(lf, lf, ACT.Exp).then_inc(exps_ready, 1)
                for b in range(TB):
                    t = aux_of(act, HALF, "pt%d" % b, half).rearrange("p (h m t) -> p h m t", h=2, m=2)
                    act.activation(probs_t[:, :, :, b * P:(b + 1) * P], t, ACT.Copy).then_inc(aux_read[4 + b], 1)
                hi_next(3)
                for j in range(2):
                    t = main_of(act, rnd, 6 + j).rearrange("p (b h v) -> p b h v", b=2, h=2)
                    act.activation(v_tok[:, 2 * j:2 * j + 2], t, ACT.Copy).then_inc(main_read[2 + j], 1)
                for h in range(2):
                    act.activation(y_hi[:, ds(half * 2 + (8 + h), 1), :], aux_of(act, HALF, "pv%d" % h, half),
                                   ACT.Copy).then_inc(attn_hi, 1)
                hi_next(4)
                act.wait_ge(operands, half * 7 + 7)
                for h in range(2):
                    act.activation(silu_g[:, h, :], main_of(act, rnd, 8 + h), ACT.Sigmoid).then_inc(sig_g, 1)
                for h in range(2):
                    t = aux_of(act, HALF, "ko%d" % h, half).rearrange("p (b f) -> p b f", b=TB)
                    act.activation(kout_t[:, h], t, ACT.Copy).then_inc(aux_read[6 + h], 1)
                hi_next(5)
                for h in range(2):
                    act.activation(conv_u[:, h, :], main_of(act, rnd, 10 + h), ACT.Copy)\
                        .then_inc(main_read[2 + h], 1)
                hi_next(6)
                hi_next(7)
                for h in range(2):
                    act.activation(o_sq[:, h, :], aux_of(act, HALF, "out%d" % h, half), ACT.Square)\
                        .then_inc(sq_ready, 1)
                for h in range(2):
                    main_copied(act, rnd, 14 + h)
                    act.activation(y_hi[:, ds(half * 2 + h, 1), :], conv_y[:, h, :], ACT.Copy)\
                        .then_inc(conv_hi, 1)
                for h in range(2):
                    act.activation(o_rstd[:, h, :], aux_of(act, HALF, "ms%d" % h, half), ACT.Ln,
                                   bias=eps[:, 1:2], scale=1.0 / P).then_inc(aux_read[6 + h], 1)
                for h in range(2):
                    aux_copied(act, HALF, "ms%d" % h, half)
                    act.activation(o_rstd[:, h, :], o_rstd[:, h, :], ACT.Exp, scale=-0.5)\
                        .then_inc(rstd_ready, 1)
                for h in range(2):
                    act.wait_ge(hgrn_ready, half * 2 + (h + 1))
                    act.activation(y_hi[:, ds(half * 2 + (4 + h), 1), :], o_norm[:, h, :], ACT.Copy)\
                        .then_inc(hgrn_hi, 1)

            def gates(i, last):
                rnd = gate_round(i)
                s0 = i * N_GATE + S_GATE
                free = {0: 0, 1: 2, 2: 4, 3: 8, 4: 10, 5: 12}

                def hi_gate(r):
                    hi(s0 + (r + 2), (r + 2) % 3, rnd * MAIN + free[r])

                for h in range(2):
                    for j in range(2):
                        hi_gate(3 * h + j)
                        if j == 0:
                            act.wait_ge(merge_done, i * 8 + (4 * h + 1))
                        for t in (2 * j, 2 * j + 1):
                            act.activation(tiles4[:, t, :], main_of(act, rnd, 8 * h + t), ACT.Sigmoid,
                                           bias=par[:, ds(i * 8 + (4 * h + t), 1)]).then_inc(main_read[t], 1)
                    if last and h == 1:
                        merged_parts(0)
                    hi_gate(3 * h + 2)

            def merged_parts(h):
                for k in range(4 * h, 4 * h + 4):
                    act.wait_ge(merge_done, 1 + 2 * KD + k + 1)
                    act.activation(y_hi[:, k, :], merged[:, k, :], ACT.Copy).then_inc(merged_hi, 1)

            with act.Fori(0, 2) as i:
                gates(i, False)
            gates(2, True)
            hi(S_OUT + 2, 3)
            merged_parts(1)
            hi(S_OUT + 3, 2, OUT_ROUND * MAIN)

            def norm(n):
                act.wait_ge(var_ready, n + 1)
                act.activation(lnw[:, 0:1], mv[:, 1:2], ACT.Sqrt, bias=eps[:, 0:1]).then_inc(std_ready, 1)

            def x1_parts(b):
                for j in range(2):
                    t = aux_of(act, LNT, "x%d%d" % (b, j)).rearrange("p (k t) -> p k t", k=4)
                    act.activation(x_hi[:, 4 * j:4 * j + 4, b * P:(b + 1) * P], t, ACT.Copy).then_inc(x1_hi, 1)

            norm(0)
            norm(1)
            x1_parts(0)
            norm(2)
            x1_parts(1)
            hi(S_MLP, 0, OUT_ROUND * MAIN + 7)
            hi(S_MLP + 1, 1, OUT_ROUND * MAIN + 7)
            norm(3)
            x1_parts(2)
            x1_parts(3)

            def mlp(g, last):
                rnd = mlp_round(g)
                s0 = g * N_MLP + S_MLP
                m0 = rnd * MAIN

                def hidden(u):
                    act.activation(tiles4[:, u % 2, :], main_of(act, rnd, u), ACT.Relu)\
                        .then_inc(main_read[u % MAIN], 1)
                    main_copied(act, rnd, u)
                    act.activation(y_hi[:, u, :], tiles4[:, u % 2, :], ACT.Square).then_inc(h_hi, 1)

                for j in range(4):
                    if j < 2:
                        hi(s0 + (j + 2), j + 2, m0)
                    elif j == 2:
                        hi(s0 + 4, 0, m0 + 2)
                    else:
                        hi(s0 + 5, 1, m0 + 4)
                        hi(s0 + 6, 2, m0 + 6)
                    for u in (2 * j, 2 * j + 1):
                        if u >= 2:
                            act.wait_ge(h_split, g * 8 + (u - 1))
                        elif u == 0:
                            act.wait_ge(slab_lo, s0 + 3)
                        hidden(u)
                hi(s0 + 7, 3, m0 + 8)
                if not last:
                    hi(s0 + 8, 0, m0 + 15)
                    hi(s0 + 9, 1, m0 + 15)
                else:
                    for b in range(TB):
                        norm(TB + b)

            with act.Fori(0, G_MLP - 1) as g:
                mlp(g, False)
            mlp(G_MLP - 1, True)

        @block.vector
        def _(dve):
            raw_slot = [0]

            def lo(s, slot):
                r = raw_slot[0]
                dve.wait_ge(slab_hi, s + 1)
                dve.tensor_tensor(w_lo[:, slot, :], raw[:, r, :], w_hi[:, slot, :].bitcast(F32), ALU.subtract)\
                    .then_inc(slab_lo, 1)
                raw_slot[0] = 1 - r

            def low_of(dst, src, high):
                return dve.tensor_tensor(dst, src, high.bitcast(F32), ALU.subtract)

            for j in range(4):
                if j == 3:
                    dve.wait_ge(front_hi, 1)
                    part = slice(0, SLAB // 2)
                    low_of(w_lo[:, 0, part], raw[:, 0, part], w_hi[:, 0, part]).then_inc(front_lo, 1)
                dve.wait_ge(transposed_hi, j + 1)
                src = bank[PRO.bank["t%d" % j]].rearrange("p (k m) -> p k m", k=2)
                low_of(memt_lo[:, 2 * j:2 * j + 2, :], src, memt_hi[:, 2 * j:2 * j + 2, :])\
                    .then_inc(aux_read[PRO.bank["t%d" % j]], 1)
            dve.wait_ge(slab_hi, 1)
            part = slice(SLAB // 2, SLAB)
            low_of(w_lo[:, 0, part], raw[:, 0, part], w_hi[:, 0, part]).then_inc(slab_lo, 1)
            raw_slot[0] = 1
            lo(1, 1)
            def x_parts(ks):
                for k in ks:
                    n = "t%d" % (4 + k)
                    dve.wait_ge(transposed_hi, 4 + k + 1)
                    low_of(x_lo[:, k, :], bank[PRO.bank[n]], x_hi[:, k, :]).then_inc(aux_read[PRO.bank[n]], 1)

            lo(2, 2)
            x_parts(range(0, 4))
            lo(3, 3)
            x_parts(range(4, KD))
            lo(4, 0)
            lo(5, 1)
            dve.tensor_copy(par[:], aux_of(dve, PRO, "t12")[:, 0:41]).then_inc(aux_read[4], 1)
            aux_copied(dve, PRO, "t12")
            lb_raw = par[:, LB:LB + HEADS]
            dve.tensor_tensor(lbw[:, 0, :], lb_raw, lb_raw, ALU.subtract).then_inc(lb_diff, 1)
            dve.wait_ge(lb_exp, 1)
            dve.reciprocal(lbw[:, 2, :], lbw[:, 1, :]).then_inc(dve_chain, 1)
            dve.wait_ge(dve_chain, 1)
            dve.tensor_tensor(lbw[:, 3, :], lbw[:, 1, :], lbw[:, 2, :], ALU.mult).then_inc(dve_chain, 1)
            dve.wait_ge(dve_chain, 2)
            dve.tensor_tensor(lbw[:, 4, :], lbw[:, 3, :], lbw[:, 3, :], ALU.subtract).then_inc(dve_chain, 1)
            dve.wait_ge(dve_chain, 3)
            dve.tensor_scalar(lbw[:, 5, :], lbw[:, 4, :], -1.0, 1.0, ALU.mult, ALU.add).then_inc(lb_ready, 1)
            dve.wait_ge(consts_ready, 1)
            dve.wait_ge(lb_ready, 1)

            CHAIN_HALF = 11

            with dve.Fori(0, 2) as half:
                s0 = half * N_PROJ + S_PROJ
                rnd = proj_round(half)
                chain = [0]

                def link(ins):
                    ins.then_inc(dve_chain, 1)
                    chain[0] += 1
                    return chain[0]

                def linked(n):
                    dve.wait_ge(dve_chain, half * CHAIN_HALF + (3 + n))

                def omlb(h):
                    return lbw[:, 5, ds(half * 2 + h, 1)]

                lo(s0 + 2, 2)
                lo(s0 + 3, 3)
                for b in range(TB):
                    t = aux_of(dve, HALF, "as%d" % b, half).rearrange("p (h m) -> p h m", h=2)
                    n = link(dve.tensor_reduce(smx[:, 0, b, :], t, AX_X, ALU.max))
                    linked(n)
                    dve.tensor_scalar(smx[:, 1, b, :], smx[:, 0, b, :], -SCALE, None, ALU.mult)\
                        .then_inc(negmax_ready, 1)
                for h in range(2):
                    dve.wait_ge(logf_ready, half * 2 + (h + 1))
                    n = link(dve.tensor_tensor_scan(bc[:, h, :], scan_keep[:], lf[:, h, :], 0.0,
                                                    ALU.mult, ALU.add))
                linked(n)
                b3 = chunks(bc)
                mid = b3[:, :, C // 2 - 1:C // 2].to_broadcast((P, 2 * NCH, C))
                end = b3[:, :, C - 1:C].to_broadcast((P, 2 * NCH, C))
                dve.tensor_tensor(chunks(aa), b3, mid, ALU.subtract).then_inc(diffs_ready, 1)
                dve.tensor_tensor(chunks(lf), end, b3, ALU.subtract).then_inc(diffs_ready, 1)
                for b in range(TB):
                    aux_copied(dve, HALF, "as%d" % b, half)
                n = link(dve.reciprocal(smx[:, 3], smx[:, 2]))
                linked(n)
                for b in range(TB):
                    for h in range(2):
                        pr = dve.tensor_scalar(probs[:, b, h, :], probs[:, b, h, :], smx[:, 3, b, h:h + 1],
                                               None, ALU.mult)
                    pr.then_inc(probs_ready, 1)
                lo(s0 + 4, 0)
                for h in range(2):
                    dve.wait_ge(sig_q, half * 2 + (h + 1))
                    dve.tensor_tensor(qq[:, h, :], qq[:, h, :], bank[h], ALU.mult).then_inc(main_read[h], 1)
                lo(s0 + 5, 1)
                dve.wait_ge(exps_ready, half * 4 + 4)
                for h in range(2):
                    dve.scalar_tensor_tensor(lf[:, h, :], kk[:, h, :], omlb(h), lf[:, h, :], ALU.mult, ALU.mult)\
                        .then_inc(operands, 1)
                for h in range(2):
                    dve.scalar_tensor_tensor(aa[:, h, :], kk[:, h, :], omlb(h), aa[:, h, :], ALU.mult, ALU.mult)\
                        .then_inc(operands, 1)
                main_copied(dve, rnd, 4)
                main_copied(dve, rnd, 5)
                dve.tensor_tensor(ee, ee, qq, ALU.mult).then_inc(operands, 1)
                dve.tensor_tensor(qq, qq, bc, ALU.mult).then_inc(operands, 1)
                dve.tensor_copy(decay[:].rearrange("p h n -> p (h n)").unsqueeze(2), b3[:, :, C - 1:C])\
                    .then_inc(operands, 1)
                for h in range(2):
                    dve.wait_ge(attn_hi, half * 2 + (h + 1))
                    r = ds(half * 2 + (8 + h), 1)
                    low_of(y_lo[:, r, :], bank[4 + h].unsqueeze(1), y_hi[:, r, :]).then_inc(aux_read[4 + h], 1)
                lo(s0 + 6, 2)
                for h in range(2):
                    aux_of(dve, HALF, "sc%d" % h, half)
                    dve.wait_ge(sig_g, half * 2 + (h + 1))
                    dve.tensor_tensor(silu_g[:, h, :], silu_g[:, h, :], bank[h], ALU.mult)\
                        .then_inc(main_read[h], 1)
                for h in range(2):
                    t = bank[4 + h].rearrange("p (b t) -> p b t", b=TB)
                    for q in range(QD):
                        part = slice(q * C, (q + 1) * C)
                        cp = dve.copy_predicated(sc_diag[part, h, :, part], causal[part], t[part, :, part])
                    cp.then_inc(aux_read[4 + h], 1)
                lo(s0 + 7, 3)
                dve.wait_ge(operands, half * 7 + 7)

                def carry(b):
                    aux_of(dve, HALF, "kv%d1" % b, half)
                    if b:
                        for h in range(2):
                            aux_copied(dve, HALF, "kv%d%d" % (b - 1, h), half)
                    for q in range(QD):
                        n = b * QD + q
                        if n == NCH - 1:
                            continue
                        last = q == QD - 1 or n == NCH - 2
                        for h in range(2):
                            kv = bank[6 + h][:, q * P:(q + 1) * P]
                            dst = states[:, h, (n + 1) % 8, :]
                            if n == 0:
                                st = dve.tensor_copy(dst, kv)
                            else:
                                st = dve.scalar_tensor_tensor(dst, states[:, h, n % 8, :], decay[:, h, n:n + 1],
                                                              kv, ALU.mult, ALU.add)
                            if last:
                                st.then_inc(aux_read[6 + h], 1)
                            else:
                                st.then_inc(state_step, 1)
                                steps[0] += 1
                        if not last:
                            dve.wait_ge(state_step, half * 22 + steps[0])

                steps = [0]
                carry(0)
                carry(1)
                lo(s0 + 8, 0)
                for h in range(2):
                    main_copied(dve, rnd, 10 + h)
                    dve.tensor_tensor(conv_u[:, h, :], conv_u[:, h, :], main_of(dve, rnd, 12 + h), ALU.mult)\
                        .then_inc(main_read[h], 1)
                    if h == 0:
                        dve.wait_ge(out_block, half * 3 + 2)
                        carry(2)
                for h in range(2):
                    main_copied(dve, rnd, 12 + h)

                    def tap(n, h=h):
                        return par[:, ds(half * 2 + (CONV_W + 4 * n + h), 1)]

                    n = link(dve.tensor_scalar(conv_y[:, h, :], conv_u[:, h, :], tap(2), None, ALU.mult))
                    for back in (1, 2):
                        linked(n)
                        st = dve.scalar_tensor_tensor(conv_y[:, h, back:T], conv_u[:, h, 0:T - back],
                                                      tap(2 - back), conv_y[:, h, back:T], ALU.mult, ALU.add)
                        if back == 1:
                            n = link(st)
                        else:
                            st.then_inc(conv_tapped, 1)
                carry(3)
                lo(s0 + 9, 1)
                for h in range(2):
                    dve.wait_ge(conv_tapped, half * 2 + (h + 1))
                    t = main_of(dve, rnd, 14 + h)
                    dve.tensor_tensor(conv_y[:, h, :], conv_y[:, h, :], t, ALU.mult).then_inc(main_read[2 + h], 1)
                for h in range(2):
                    r = ds(half * 2 + h, 1)
                    dve.wait_ge(conv_hi, half * 2 + (h + 1))
                    low_of(y_lo[:, r, :], conv_y[:, h:h + 1, :], y_hi[:, r, :]).then_inc(branch_split, 1)
                for h in range(2):
                    dve.wait_ge(rstd_ready, half * 2 + (h + 1))
                    dve.scalar_tensor_tensor(o_norm[:, h, :], bank[4 + h], par[:, NORM_W:NORM_W + 1],
                                             o_rstd[:, h, :], ALU.mult, ALU.mult).then_inc(aux_read[4 + h], 1)
                for h in range(2):
                    aux_copied(dve, HALF, "out%d" % h, half)
                    main_copied(dve, rnd, 8 + h)
                    dve.tensor_tensor(o_norm[:, h, :], o_norm[:, h, :], silu_g[:, h, :], ALU.mult)\
                        .then_inc(hgrn_ready, 1)
                for h in range(2):
                    r = ds(half * 2 + (4 + h), 1)
                    dve.wait_ge(hgrn_hi, half * 2 + (h + 1))
                    low_of(y_lo[:, r, :], o_norm[:, h:h + 1, :], y_hi[:, r, :]).then_inc(branch_split, 1)
                assert chain[0] <= CHAIN_HALF, chain
                assert chain[0] == CHAIN_HALF and steps[0] == 22, (chain, steps)

            def gates(i, last):
                rnd = gate_round(i)
                s0 = i * N_GATE + S_GATE
                for h in range(2):
                    for j in range(3):
                        r = 3 * h + j + 2
                        lo(s0 + r, r % 3)
                        if last and h == 1 and j == 1:
                            merged_parts(0)
                    dve.wait_ge(merge_done, i * 8 + (4 * h + 1))
                    for t in range(4):
                        main_copied(dve, rnd, 8 * h + t)
                        src = main_of(dve, rnd, 8 * h + 4 + t)
                        dve.tensor_tensor(tiles4[:, t, :], tiles4[:, t, :], src, ALU.mult)\
                            .then_inc(main_read[t], 1)
                        main_copied(dve, rnd, 8 * h + 4 + t)
                        k = 4 * h + t
                        dve.tensor_tensor(merged[:, k, :], merged[:, k, :], tiles4[:, t, :], ALU.add)\
                            .then_inc(merge_done, 1)

            def merged_parts(h):
                for k in range(4 * h, 4 * h + 4):
                    dve.wait_ge(merged_hi, k + 1)
                    low_of(y_lo[:, k, :], merged[:, k, :], y_hi[:, k, :]).then_inc(merged_split, 1)

            with dve.Fori(0, 2) as i:
                gates(i, False)
            gates(2, True)
            merged_parts(1)
            lo(S_OUT + 2, 3)
            lo(S_OUT + 3, 2)

            ln_chain = [0]

            def ln_link(ins):
                ins.then_inc(ln_step, 1)
                ln_chain[0] += 1
                dve.wait_ge(ln_step, ln_chain[0])

            def half_of(b, e):
                return resid[:, b, e * WID:(e + 1) * WID]

            def norm(n, done):
                b = n % TB
                p = 2 * (n // TB)
                dve.bn_aggr(mv[:], stats[:].rearrange("p e s -> p (e s)")).then_inc(var_ready, 1)
                dve.wait_ge(var_ready, n + 1)
                for e in range(2):
                    dve.scalar_tensor_tensor(half_of(b, e), half_of(b, e), mv[:, 0:1],
                                             ln_par[:, p, e * WID:(e + 1) * WID], ALU.subtract, ALU.mult)
                dve.wait_ge(std_ready, n + 1)
                ln_link(dve.reciprocal(lnw[:, 1:2], lnw[:, 0:1]))
                for e in range(2):
                    dve.scalar_tensor_tensor(half_of(b, e), half_of(b, e), lnw[:, 1:2],
                                             ln_par[:, p + 1, e * WID:(e + 1) * WID], ALU.mult, ALU.add)\
                        .then_inc(done, 1)

            def stats_of(rnd, t, b, e):
                main_copied(dve, rnd, t)
                st = dve.bn_stats(stats[:, e, :], half_of(b, e))
                if e == 1:
                    ln_link(st)

            def x1_parts(b):
                for j in range(2):
                    dve.wait_ge(x1_hi, 2 * b + j + 1)
                    n = "x%d%d" % (b, j)
                    part = (slice(None), slice(4 * j, 4 * j + 4), slice(b * P, (b + 1) * P))
                    low_of(x_lo[part], bank[LNT.bank[n]].rearrange("p (k t) -> p k t", k=4), x_hi[part])\
                        .then_inc(aux_read[LNT.bank[n]], 1)

            dve.wait_ge(x_again, 16)
            dve.wait_ge(ln_landed, 64)

            def mixed(b, e):
                w = 2 * b + e
                z = resid[:, b, e * WID:(e + 1) * WID]
                dve.scalar_tensor_tensor(z, z, ALPHA, main_of(dve, OUT_ROUND, w), ALU.mult, ALU.add)\
                    .then_inc(main_read[w % MAIN], 1)

            for b in range(TB):
                mixed(b, 0)
                stats_of(OUT_ROUND, 2 * b, b, 0)
                if b == TB - 1:
                    lo(S_MLP, 0)
                    lo(S_MLP + 1, 1)
                mixed(b, 1)
                stats_of(OUT_ROUND, 2 * b + 1, b, 1)
                norm(b, x1_ready)
                if b:
                    x1_parts(b - 1)
            x1_parts(TB - 1)

            def mlp(g, last):
                rnd = mlp_round(g)
                s0 = g * N_MLP + S_MLP
                for j in range(4):
                    for s in ((2,), (3,), (4,), (5, 6))[j]:
                        lo(s0 + s, s % 4)
                    for u in (2 * j, 2 * j + 1):
                        main_copied(dve, rnd, u)
                        r, h = tiles4[:, u % 2, :], tiles4[:, 2 + u % 2, :]
                        dve.tensor_tensor(h, r, r, ALU.mult).then_inc(h_made, 1)
                        dve.wait_ge(h_made, g * 8 + (u + 1))
                        dve.wait_ge(h_hi, g * 8 + (u + 1))
                        low_of(y_lo[:, u, :], h, y_hi[:, u, :]).then_inc(h_split, 1)
                lo(s0 + 7, 3)
                for w in range(2 * TB):
                    b, e = divmod(w, 2)
                    z = resid[:, b, e * WID:(e + 1) * WID]
                    dve.wait_ge(resid_ready, b + 1)
                    dve.wait_ge(main_read[w % MAIN], rnd + ((8 + w) // MAIN))
                    dve.tensor_tensor(z, z, main_of(dve, rnd, 8 + w), ALU.add).then_inc(main_read[w % MAIN], 1)
                    if not last and w == 2 * TB - 2:
                        lo(s0 + 8, 0)
                        lo(s0 + 9, 1)
                    if last:
                        stats_of(rnd, 8 + w, b, e)
                        if e == 1:
                            norm(TB + b, y_ready)

            with dve.Fori(0, G_MLP - 1) as g:
                mlp(g, False)
            mlp(G_MLP - 1, True)

        @block.tensor
        def _(pe):
            def begin(rnd, t):
                r = rnd + t // MAIN
                if not isinstance(r, int) or r > 0:
                    pe.wait_ge(main_read[t % MAIN], r)
                return bank[t % MAIN]

            def begin_aux(phase, name, it=0):
                n = phase.earlier(name, it)
                if not isinstance(n, int) or n > 0:
                    pe.wait_ge(aux_read[phase.bank[name]], n)
                return bank[phase.bank[name]]

            def slab(s):
                pe.wait_ge(slab_lo, s + 1)

            def three(dst, a, b, first, last):
                pe.matmul(dst, a[0], b[0], start=first, stop=False)
                pe.matmul(dst, a[0], b[1], start=False, stop=False)
                return pe.matmul(dst, a[1], b[0], start=False, stop=last)

            def w_part(slot, at, n):
                return w_hi[:, slot, at:at + n], w_lo[:, slot, at:at + n]

            def both(hi_, lo_, *at):
                return hi_[at], lo_[at]

            ALL = slice(None)

            pe.wait_ge(ident_ready, 1)
            for j in range(4):
                if j % 2 == 0:
                    pe.wait_ge(mem_landed[j // 2], 16)
                t = begin_aux(PRO, "t%d" % j)
                for k in range(2):
                    for b in range(2):
                        c = (2 * j + k) * P
                        tr = pe.transpose(t[:, (2 * k + b) * P:(2 * k + b + 1) * P], mem_tok[:, b, c:c + P],
                                          ident[:])
                tr.then_inc(aux_done, 1)

            def x_transposed(ks):
                for k in ks:
                    t = begin_aux(PRO, "t%d" % (4 + k))
                    for b in range(TB):
                        tr = pe.transpose(t[:, b * P:(b + 1) * P], x_tok[:, b, k * P:(k + 1) * P], ident[:])
                    tr.then_inc(aux_done, 1)

            for s in range(4):
                if s == 2:
                    pe.wait_ge(x_landed, 16)
                    x_transposed(range(0, 4))
                if s:
                    slab(s)
                for c in range(2):
                    if s == 2 and c == 1:
                        x_transposed(range(4, KD))
                    t = begin(0, 2 * s + c)[:, 0:M]
                    for k in range(KD):
                        if s == 0 and c == 0:
                            if k == 0:
                                pe.wait_ge(front_lo, 1)
                            if k == KD // 2:
                                slab(0)
                            if k % 2 == 0:
                                aux_copied(pe, PRO, "t%d" % (k // 2))
                        if s < 2:
                            mm = three(t, w_part(s, k * 256 + c * P, P), both(memt_hi, memt_lo, ALL, k),
                                       k == 0, k == KD - 1)
                        else:
                            mm = three(t, both(memt_hi, memt_lo, ALL, k, slice(c * P, (c + 1) * P)),
                                       w_part(s, k * 256, 256), k == 0, k == KD - 1)
                    mm.then_inc(tile_done, 1)
            pe.wait_ge(small_landed, 64)
            pe.transpose(begin_aux(PRO, "t12")[:, 0:41], par_rows, ident[0:41, 0:41]).then_inc(aux_done, 1)

            def feature_part(dst, tokens, slot, c):
                for k in range(KD):
                    mm = three(dst[:, tokens], w_part(slot, k * 256 + c * P, P), both(x_hi, x_lo, ALL, k, tokens),
                               k == 0, k == KD - 1)
                return mm

            def feature_tile(rnd, t, slot, c):
                feature_part(begin(rnd, t), slice(0, T), slot, c).then_inc(tile_done, 1)

            for k in range(4, 12):
                aux_copied(pe, PRO, "t%d" % k)

            with pe.Fori(0, 2) as half:
                rnd = proj_round(half)
                s0 = half * N_PROJ + S_PROJ

                def blk(b):
                    return slice(b * P, (b + 1) * P)

                def slab_tiles(j):
                    slab(s0 + j)
                    for c in range(2):
                        feature_tile(rnd, 2 * j + c, j % 4, c)

                slab_tiles(0)
                slab_tiles(1)
                for h in range(2):
                    main_copied(pe, rnd, h)
                for b in range(TB):
                    t = begin_aux(HALF, "as%d" % b, half)
                    for h in range(2):
                        mm = pe.matmul(t[:, h * M:(h + 1) * M], q_mem[:, h, blk(b)],
                                       mem_k[:, ds(half * 2 + h, 1), :], start=True, stop=True)
                    mm.then_inc(aux_done, 1)
                slab_tiles(2)
                for b in range(TB):
                    pe.wait_ge(probs_ready, half * TB + (b + 1))
                    t = begin_aux(HALF, "pt%d" % b, half)
                    for h in range(2):
                        for m in range(2):
                            tr = pe.transpose(t[:, blk(2 * h + m)], probs[:, b, h, blk(m)], ident[:])
                    tr.then_inc(aux_done, 1)
                slab(s0 + 3)
                for j in range(2):
                    dst = begin(rnd, 6 + j)
                    for b in range(2):
                        for k in range(KD):
                            mm = three(dst[:, b * 256:(b + 1) * 256],
                                       both(x_hi, x_lo, ALL, k, blk(2 * j + b)), w_part(3, k * 256, 256),
                                       k == 0, k == KD - 1)
                    mm.then_inc(tile_done, 1)
                pe.wait_ge(vhalf_ready, half + 1)
                for b in range(TB):
                    aux_copied(pe, HALF, "pt%d" % b, half)
                for h in range(2):
                    t = begin_aux(HALF, "pv%d" % h, half)
                    for m in range(2):
                        mm = pe.matmul(t, mem_v_half[:, m, blk(h)], probs_t[:, h, m, :], start=m == 0, stop=m == 1)
                    mm.then_inc(aux_done, 1)
                slab_tiles(4)
                pe.wait_ge(operands, half * 7 + 2)
                for h in range(2):
                    t = begin_aux(HALF, "ko%d" % h, half)
                    for b in range(TB):
                        tr = pe.transpose(t[:, blk(b)], lf[:, h, blk(b)], ident[:])
                    tr.then_inc(aux_done, 1)
                pe.wait_ge(operands, half * 7 + 5)
                for h in range(2):
                    t = begin_aux(HALF, "sc%d" % h, half)
                    for b in range(TB):
                        mm = pe.matmul(t[:, blk(b)], aa[:, h, blk(b)], ee[:, h, blk(b)], start=True, stop=True)
                    mm.then_inc(aux_done, 1)

                def kv(b):
                    pe.wait_ge(v_diag_ready, half * TB + (b + 1))
                    for h in range(2):
                        pe.matmul(begin_aux(HALF, "kv%d%d" % (b, h), half), kout_t[:, h, b, :],
                                  v_diag[:, b % 2, h].rearrange("p c v -> p (c v)"), start=True, stop=True)\
                            .then_inc(aux_done, 1)

                def outs(b):
                    if b == 0:
                        pe.wait_ge(operands, half * 7 + 7)
                    for h in range(2):
                        if b == 0:
                            begin_aux(HALF, "out%d" % h, half)
                        t = bank[4 + h]
                        aux_copied(pe, HALF, "kv%d%d" % (b, h), half)
                        pe.matmul(t[:, blk(b)], v_tok[:, b, h, :], sc_diag[:, h, b, :], start=b == 0, stop=False)
                        for q in range(QD):
                            n = b * QD + q
                            if n:
                                mm = pe.matmul(t[:, n * C:(n + 1) * C], states[:, h, n % 8, :],
                                               qq[:, h, n * C:(n + 1) * C], start=False, stop=n == NCH - 1)
                        if b == TB - 1:
                            mm.then_inc(aux_done, 1)
                    if b < TB - 1:
                        mm.then_inc(out_block, 1)

                slab(s0 + 5)
                feature_tile(rnd, 10, 1, 0)
                kv(0)
                feature_tile(rnd, 11, 1, 1)
                kv(1)
                outs(0)
                slab(s0 + 6)
                feature_tile(rnd, 12, 2, 0)
                outs(1)
                kv(2)
                feature_tile(rnd, 13, 2, 1)
                outs(2)
                kv(3)
                slab(s0 + 7)
                feature_tile(rnd, 14, 3, 0)
                outs(3)
                feature_tile(rnd, 15, 3, 1)
                pe.wait_ge(consts_ready, 1)
                for h in range(2):
                    pe.wait_ge(sq_ready, half * 2 + (h + 1))
                    pe.matmul(begin_aux(HALF, "ms%d" % h, half), ones[:], o_sq[:, h, :], start=True, stop=True)\
                        .then_inc(aux_done, 1)

            with pe.Fori(0, 3) as i:
                rnd = gate_round(i)
                s0 = i * N_GATE + S_GATE
                for h in range(2):
                    for j in range(2):
                        r = 3 * h + j
                        slab(s0 + r)
                        for c in range(2):
                            feature_tile(rnd, 8 * h + 2 * j + c, r % 3, c)
                    slab(s0 + (3 * h + 2))
                    pe.wait_ge(branch_split, 8)
                    for c in range(4):
                        dst = begin(rnd, 8 * h + 4 + c)
                        for k in range(HEADS):
                            mm = three(dst, w_part(2, k * WID + c * P, P),
                                       both(y_hi, y_lo, ALL, ds(i * HEADS + k, 1)), k == 0, k == HEADS - 1)
                        mm.then_inc(tile_done, 1)

            def token_chunk(dst, b, e, k, slots):
                return three(dst, both(y_hi, y_lo, ALL, k, slice(b * P, (b + 1) * P)),
                             w_part(slots[e][k // 4], (k % 4) * WID, WID), k == 0, k == KD - 1)

            def token_tiles(rnd, t0, slots, first):
                for b in range(TB):
                    for e in range(2):
                        dst = begin(rnd, t0 + 2 * b + e)
                        for k in range(KD):
                            if b == 0:
                                first(e, k)
                            mm = token_chunk(dst, b, e, k, slots)
                        mm.then_inc(tile_done, 1)

            def x1_transposed(b):
                pe.wait_ge(x1_ready, 2 * (b + 1))
                for j in range(2):
                    t = begin_aux(LNT, "x%d%d" % (b, j))
                    for k in range(4):
                        c = (4 * j + k) * P
                        tr = pe.transpose(t[:, k * P:(k + 1) * P], resid[:, b, c:c + P], ident[:])
                    tr.then_inc(aux_done, 1)

            out_slots = ((0, 1), (3, 2))
            slab(S_OUT)
            for b in range(2):
                dst = begin(OUT_ROUND, 2 * b)
                for k in range(4):
                    if b == 0:
                        pe.wait_ge(merged_split, k + 1)
                    token_chunk(dst, b, 0, k, out_slots)
            for b in range(TB):
                for e in range(2):
                    begun = b < 2 and e == 0
                    dst = bank[2 * b] if begun else begin(OUT_ROUND, 2 * b + e)
                    for k in range(4 if begun else 0, KD):
                        if b == 0 and k % 4 == 0:
                            slab(S_OUT + 2 * e + k // 4)
                        if b == 0 and begun:
                            pe.wait_ge(merged_split, k + 1)
                        mm = token_chunk(dst, b, e, k, out_slots)
                    mm.then_inc(tile_done, 1)
                if b:
                    x1_transposed(b - 1)

            for b in range(2):
                for j in range(2):
                    aux_copied(pe, LNT, "x%d%d" % (b, j))
            for u in range(4):
                if u % 2 == 0:
                    slab(S_MLP + u // 2)
                if u == 3:
                    x1_transposed(TB - 1)
                feature_part(begin(mlp_round(0), u), slice(0, T // 2), u // 2, u % 2)
            for b in range(2, TB):
                for j in range(2):
                    aux_copied(pe, LNT, "x%d%d" % (b, j))
            for u in range(4):
                feature_part(bank[u], slice(T // 2, T), u // 2, u % 2).then_inc(tile_done, 1)

            def mlp(g, begun=0):
                rnd = mlp_round(g)
                s0 = g * N_MLP + S_MLP
                for j in range(begun, 4):
                    slab(s0 + j)
                    for c in range(2):
                        feature_tile(rnd, 2 * j + c, j, c)

                def first(e, k):
                    if k % 4 == 0:
                        slab(s0 + (4 + 2 * e + k // 4))
                    if e == 0:
                        pe.wait_ge(h_split, g * 8 + (k + 1))

                token_tiles(rnd, 8, ((0, 1), (2, 3)), first)

            mlp(0, 2)
            with pe.Fori(1, G_MLP) as g:
                mlp(g)


_INS = ["x", "mem", "lower_bounds", "w_in", "conv_w", "hg_norm_w", "w_mem_k", "w_mem_v", "w_branch", "b_gate",
        "w_o", "ln1_g", "ln1_b", "w_up", "w_down", "ln2_g", "ln2_b"]


def kernel(**inputs):
    import numpy as _np
    import concourse.bacc as _bacc
    from concourse import mybir as _mybir
    from concourse.bass_utils import run_bass_kernel_spmd as _run

    nc = _bacc.Bacc("TRN2", target_bir_lowering=False, num_devices=1, dynamic_dma_scratch_size=1024)
    arrays, args = {}, []
    for name in _INS:
        a = _np.ascontiguousarray(inputs[name])
        arrays[f"in_{name}_dram"] = a
        args.append(nc.dram_tensor(f"in_{name}_dram", a.shape, _mybir.dt.from_np(a.dtype), kind="ExternalInput").ap())
    args.append(nc.dram_tensor("out_dram", inputs["x"].shape, _mybir.dt.float32, kind="ExternalOutput").ap())
    build(nc, *args)
    r = _run(nc, [arrays], core_ids=[0])
    return r.results[0]["out_dram"]
```

```python
from contextlib import ExitStack

import concourse.bass as bass
from concourse import mybir

F32 = mybir.dt.float32
F32R = mybir.dt.float32r
U32 = mybir.dt.uint32
ALU = mybir.AluOpType
ACT = mybir.ActivationFunctionType
AX_X = mybir.AxisListType.X

P = 128
T = 512
D = 1024
KD = D // P
M = 256
WID = 512
HEADS = WID // P
TB = T // P
C = 32
NCH = T // C
QD = P // C
DFF = 4 * D
DEPTH = 1
ALPHA = (2.0 * DEPTH) ** 0.25
LN_EPS = 1e-5
RMS_EPS = 1e-6
SCALE = float(P) ** -0.5
SLAB = 2048
MAIN = 4

COL = dict(cb=0, cc=WID, ch=2 * WID, q=3 * WID, f=4 * WID, v=5 * WID, g=6 * WID, mq=7 * WID, gate=8 * WID)
PROJ = ["mq", "f", "q", "v", "g", "cc", "ch", "cb"]

S_PROJ, N_PROJ = 4, len(PROJ)
S_GATE, N_GATE = S_PROJ + 2 * N_PROJ, 6
S_OUT = S_GATE + 3 * N_GATE
S_MLP, N_MLP = S_OUT + 4, 8
G_MLP = DFF // D
M_PROJ, M_GATE = 8, 8 + 2 * 16
M_OUT = M_GATE + 3 * 16
M_MLP = M_OUT + 8

AUX_PRO = [("t%d" % i, 4 + i % 4) for i in range(13)]
AUX_HALF = ([("as%d" % b, 4 + b) for b in range(4)] + [("pt%d" % b, 4 + b) for b in range(4)]
            + [("pv0", 4), ("pv1", 5), ("sc0", 4), ("sc1", 5), ("ko0", 6), ("ko1", 7), ("kv0", 6), ("kv1", 7)]
            + [("out0", 4), ("out1", 5), ("ms0", 6), ("ms1", 7)])
AUX_LN = [("x%d%d" % (b, j), 4 + 2 * (b % 2) + j) for b in range(TB) for j in range(2)]


def uses(bank, seq):
    return sum(1 for _, b in seq if b == bank)


class Aux:

    def __init__(self, seq, before):
        self.seq = seq
        self.index = {n: i for i, (n, _) in enumerate(seq)}
        self.bank = dict(seq)
        self.first = sum(len(s) * r for s, r in before)
        self.before = {b: sum(uses(b, s) * r for s, r in before) for b in range(4, 8)}

    def done(self, name, it=0):
        return it * len(self.seq) + (self.first + self.index[name] + 1)

    def earlier(self, name, it=0):
        b = self.bank[name]
        return it * uses(b, self.seq) + (self.before[b] + uses(b, self.seq[:self.index[name]]))

    def read(self, name, it=0):
        return self.earlier(name, it) + 1


PRO = Aux(AUX_PRO, [])
HALF = Aux(AUX_HALF, [(AUX_PRO, 1)])
LNT = Aux(AUX_LN, [(AUX_PRO, 1), (AUX_HALF, 2)])


def build(nc, x, mem, lower_bounds, w_in, conv_w, hg_norm_w, w_mem_k, w_mem_v, w_branch, b_gate, w_o,
          ln1_g, ln1_b, w_up, w_down, ln2_g, ln2_b, out):
    ds = bass.ds
    with ExitStack() as ctx:
        def sb(name, shape, dt=F32):
            return ctx.enter_context(nc.sbuf_tensor(name, shape, dt))

        def sem(name):
            return ctx.enter_context(nc.semaphore(name))

        raw = sb("raw", [P, 2, SLAB])
        w_hi = sb("w_hi", [P, 4, SLAB], F32R)
        w_lo = sb("w_lo", [P, 4, SLAB], F32R)
        x_hi = sb("x_hi", [P, KD, T], F32R)
        x_lo = sb("x_lo", [P, KD, T], F32R)
        y_hi = sb("y_hi", [P, 3 * HEADS, T], F32R)
        y_lo = sb("y_lo", [P, 3 * HEADS, T], F32R)
        memt_hi = y_hi[:, 8:12, :].rearrange("p a (b m) -> p (a b) m", m=M)
        memt_lo = y_lo[:, 8:12, :].rearrange("p a (b m) -> p (a b) m", m=M)
        mk_hi, mk_lo = (y[:, 2, :].rearrange("p (h m) -> p h m", h=2) for y in (y_hi, y_lo))
        mv_hi, mv_lo = (y[:, 3, :].rearrange("p (m w) -> p m w", m=2) for y in (y_hi, y_lo))
        qm_hi, qm_lo = (y[:, 6:8, :] for y in (y_hi, y_lo))
        PT_ROW = (6, 7, 10, 11)
        sq_hi, sq_lo = qm_hi, qm_lo

        two = sb("two", [P, 6, 1024])
        x_tok = two[:, 0:4, :]
        mem_tok = two[:, 4:6, :]
        resid = two[:, 0:4, :]
        tiles4 = two[:, 4:6, :].rearrange("p a (b t) -> p (a b) t", t=T)

        def heads2(n):
            return two[:, n, :].rearrange("p (h t) -> p h t", h=2)

        kk, qq, lf, bc, aa, ee = (heads2(n) for n in range(6))
        silu_g = kk
        conv_u = bc
        conv_y = lf
        sq_all = qq
        o_rstd = ee
        o_norm = aa

        def chunks(buf):
            return buf.rearrange("p h (n c) -> p (h n) c", c=C)

        small = sb("small", [P, 9 * 1024])
        states = small[:, 0:768].rearrange("p (h b v) -> p h b v", h=2, v=P)
        q_block = small[:, 1024:2048].rearrange("p (h t) -> p h t", h=2)
        k_two = small[:, 2048:2560].rearrange("p (n c) -> p n c", c=2 * C)
        k_three = small[:, 2560:3328].rearrange("p (n c) -> p n c", c=3 * C)
        probs = small[:, 2048:4096].rearrange("p (b h m) -> p b h m", b=TB, h=2)
        v_tok = small[:, 4096:5120].rearrange("p (b h v) -> p b h v", b=TB, h=2)
        kout_t = small[:, 5120:6144].rearrange("p (h b f) -> p h b f", h=2, b=TB)
        par_rows = small[0:41, 5120:5248]
        sc_causal = small[:, 6144:7168].rearrange("p (h b t) -> p h b t", h=2, b=TB)
        mem_k = small[:, 7168:8192].rearrange("p (h m) -> p h m", h=HEADS)
        mem_v = small[:, 8192:9216].rearrange("p (b w) -> p b w", b=2)
        causal_f = small[:, 0:P]
        ones_f = small[:, P:2 * P]
        merged = small[:, 0:4096].rearrange("p (k t) -> p k t", k=KD)
        ln_par = small[:, 4096:8192].rearrange("p (n d) -> p n d", n=4)

        ident = sb("ident", [P, P])
        ones = sb("ones", [P, P], F32R)
        scan_keep = sb("scan_keep", [P, T], mybir.dt.uint8)
        causal = sb("causal", [P, P], U32)
        par = sb("par", [P, 41])
        CONV_W, LB, NORM_W = 24, 36, 40
        lbw = sb("lbw", [P, 6, HEADS])
        eps = sb("eps", [P, 2])
        smx = sb("smx", [P, 4, TB, 2])
        decay = sb("decay", [P, 2 * TB, QD])
        decays = sb("decays", [P, 2 * TB, QD + 1])
        stats = sb("stats", [P, 2, 6])
        mv = sb("mv", [P, 2])
        lnw = sb("lnw", [P, 2])

        bank = [ctx.enter_context(nc.psum_tensor("bank%d" % n, [P, T], F32))[:, :] for n in range(8)]

        small_landed = sem("small_landed")
        mem_landed = [sem("mem_landed0"), sem("mem_landed1")]
        front_landed = sem("front_landed")
        x_landed = sem("x_landed")
        slab_landed = [sem("slab_landed0"), sem("slab_landed1")]
        x_again = sem("x_again")
        ln_landed = sem("ln_landed")
        stored = sem("stored")
        slab_hi = sem("slab_hi")
        slab_lo = sem("slab_lo")
        tile_done = sem("tile_done")
        main_read = [sem("main_read%d" % n) for n in range(MAIN)]
        aux_done = sem("aux_done")
        aux_read = {b: sem("aux_read%d" % b) for b in range(4, 8)}
        ident_ready, consts_ready = (sem(n) for n in
            ("ident_ready", "consts_ready"))
        lb_diff, lb_exp, lb_ready = (sem(n) for n in
            ("lb_diff", "lb_exp", "lb_ready"))
        transposed_hi, front_hi, front_lo = (sem(n) for n in
            ("transposed_hi", "front_hi", "front_lo"))
        half_hi, khalf_ready, vhalf_ready = (sem(n) for n in
            ("half_hi", "khalf_ready", "vhalf_ready"))
        qm_rounded, negmax_ready, probs_ready, pt_rounded = (sem(n) for n in
            ("qm_rounded", "negmax_ready", "probs_ready", "pt_rounded"))
        attn_hi = sem("attn_hi")
        logf_ready, diffs_ready, exps_ready, sig_q = (sem(n) for n in
            ("logf_ready", "diffs_ready", "exps_ready", "sig_q"))
        sig_g, operands, state_step, sq_ready = (sem(n) for n in
            ("sig_g", "operands", "state_step", "sq_ready"))
        sq_split, rstd_ready, hgrn_ready, hgrn_hi = (sem(n) for n in
            ("sq_split", "rstd_ready", "hgrn_ready", "hgrn_hi"))
        conv_tapped, conv_hi, branch_split = (sem(n) for n in
            ("conv_tapped", "conv_hi", "branch_split"))
        merge_done, merged_hi, merged_split = (sem(n) for n in
            ("merge_done", "merged_hi", "merged_split"))
        var_ready, std_ready, x1_ready, x1_hi = (sem(n) for n in
            ("var_ready", "std_ready", "x1_ready", "x1_hi"))
        resid_ready, y_ready = (sem(n) for n in
            ("resid_ready", "y_ready"))
        h_hi, h_made, h_split = (sem(n) for n in
            ("h_hi", "h_made", "h_split"))
        dve_chain, ln_step, pool_chain = (sem(n) for n in
            ("dve_chain", "ln_step", "pool_chain"))

        OPERANDS = 10

        def proj_round(half):
            return half * 4 + 2

        def gate_round(i):
            return i * 4 + 10

        OUT_ROUND = 22

        def mlp_round(g):
            return g * 4 + 24

        def main_of(eng, rnd, t):
            eng.wait_ge(tile_done, rnd * MAIN + (t + 1))
            return bank[t % MAIN]

        def main_copied(eng, rnd, t):
            eng.wait_ge(main_read[t % MAIN], rnd + (t // MAIN + 1))

        def aux_of(eng, phase, name, it=0):
            eng.wait_ge(aux_done, phase.done(name, it))
            return bank[phase.bank[name]]

        def aux_copied(eng, phase, name, it=0):
            eng.wait_ge(aux_read[phase.bank[name]], phase.read(name, it))

        block = ctx.enter_context(nc.Block())

        def rows(w):
            return w.rearrange("(k p) c -> p k c", p=P)

        win, wup, wdn, wout = rows(w_in[0]), rows(w_up[0]), rows(w_down[0]), rows(w_o[0])
        win_256 = w_in[0].rearrange("(k p) (n c) -> p k n c", p=P, c=256)
        wmk, wmv = rows(w_mem_k[0]), rows(w_mem_v[0])
        wbr = w_branch[0].rearrange("i (k p) c -> p (i k) c", p=P)
        out_t = out[0].rearrange("(b p) d -> b p d", p=P)
        x_t = x[0].rearrange("(b p) d -> p b d", p=P)

        @block.sync
        def _(sp):
            def load(s, r, src, k):
                if not isinstance(s, int) or s >= 2:
                    sp.wait_ge(slab_lo, s - 1)
                if len(src.shape) == 4:
                    src = src.rearrange("p k n c -> p k (n c)")
                sp.dma_start(raw[:, r, :].rearrange("p (k c) -> p k c", k=k), src).then_inc(slab_landed[r], 16)

            for e in range(2):
                part = slice(e * WID, (e + 1) * WID)
                sp.dma_start(mem_tok[:, :, part], mem[0].rearrange("(b p) d -> p b d", p=P)[:, :, part])\
                    .then_inc(mem_landed[e], 16)
            for part in (slice(0, KD // 2), slice(KD // 2, KD)):
                sp.dma_start(raw[:, 0, :].rearrange("p (k c) -> p k c", k=KD)[:, part], wmk[:, part, 0:256])\
                    .then_inc(front_landed if part.start == 0 else slab_landed[0], 16)
            load(1, 1, wmk[:, :, 256:512], KD)
            sp.dma_start(x_tok, x_t).then_inc(x_landed, 16)
            for to, rows_of in ((par_rows[0:24], b_gate[0].rearrange("(r p) -> r p", p=P)),
                                (par_rows[24:36], conv_w[0].rearrange("t (r p) -> (t r) p", p=P)),
                                (par_rows[36:40], lower_bounds[0].rearrange("(r p) -> r p", p=P)),
                                (par_rows[40:41], hg_norm_w)):
                sp.dma_start(to, rows_of).then_inc(small_landed, 16)
            load(2, 0, wmv[:, :, 0:256], KD)
            load(3, 1, wmv[:, :, 256:512], KD)
            with sp.Fori(0, 2) as half:
                for j, name in enumerate(PROJ):
                    n = half + COL[name] // 256
                    load(half * N_PROJ + (S_PROJ + j), j % 2, win_256[:, :, ds(n, 1), :], KD)
            with sp.Fori(0, 3) as i:
                for h in range(2):
                    for j in range(2):
                        load(i * N_GATE + (S_GATE + 3 * h + j), (3 * h + j) % 2,
                             win[:, :, ds(i * D + (COL["gate"] + h * WID + j * 256), 256)], KD)
                    load(i * N_GATE + (S_GATE + 3 * h + 2), (3 * h + 2) % 2,
                         wbr[:, ds(i * HEADS, HEADS), h * WID:(h + 1) * WID], HEADS)
            sp.wait_ge(branch_split, 8)
            sp.dma_start(resid, x_t).then_inc(x_again, 16)
            for n, v in enumerate((ln1_g, ln1_b, ln2_g, ln2_b)):
                sp.dma_start(ln_par[:, n, :], v.to_broadcast((P, D))).then_inc(ln_landed, 16)
            for e in range(2):
                for h in range(2):
                    load(S_OUT + 2 * e + h, h, wout[:, 4 * h:4 * h + 4, e * WID:(e + 1) * WID], 4)
            with sp.Fori(0, G_MLP) as g:
                for j in range(4):
                    load(g * N_MLP + (S_MLP + j), j % 2, wup[:, :, ds(g * D + j * 256, 256)], KD)
                for e in range(2):
                    for h in range(2):
                        load(g * N_MLP + (S_MLP + 4 + 2 * e + h), h,
                             wdn[:, ds(g * KD + 4 * h, 4), e * WID:(e + 1) * WID], 4)
            for b in range(TB):
                for e in range(2):
                    part = slice(e * WID, (e + 1) * WID)
                    sp.wait_ge(y_ready, 2 * b + (e + 1))
                    sp.dma_start(out_t[b][:, part], resid[:, b, part]).then_inc(stored, 16)
            sp.wait_ge(stored, 16 * 2 * TB)

        @block.gpsimd
        def _(pool):
            chain = [0]

            def after(ins):
                ins.then_inc(pool_chain, 1)
                chain[0] += 1
                pool.wait_ge(pool_chain, chain[0])

            after(pool.memset(ident[:], 0.0))
            pool.affine_select(out=ident[:], in_=ident[:], compare_op=ALU.not_equal, fill=1.0, base=0,
                               pattern=[[-1, P]], channel_multiplier=1).then_inc(ident_ready, 1)
            after(pool.memset(ones_f, 1.0))
            pool.tensor_copy(ones[:], ones_f)
            pool.memset(scan_keep[:], 1)
            pool.memset(eps[:, 0:1], LN_EPS)
            pool.memset(eps[:, 1:2], RMS_EPS)
            pool.memset(sc_causal, 0.0)
            pool.memset(decays[:, :, 0:1], 1.0)
            after(pool.memset(causal_f, 0.0))
            pool.memset(scan_keep[:].rearrange("p (n c) -> p n c", c=C)[:, :, 0:1], 0)
            after(pool.affine_select(out=causal_f, in_=causal_f, compare_op=ALU.is_gt, fill=1.0, base=0,
                                     pattern=[[-1, P]], channel_multiplier=1))
            pool.tensor_copy(causal[:], causal_f).then_inc(consts_ready, 1)

            for half in range(2):
                def parts(src, high, low, n, ready):
                    pool.tensor_copy(high, src).then_inc(half_hi, 1)
                    pool.wait_ge(half_hi, n)
                    pool.tensor_tensor(low, src, high.bitcast(F32), ALU.subtract).then_inc(ready, 1)

                if half == 0:
                    for t in range(4):
                        main_copied(pool, 0, t)
                else:
                    pool.wait_ge(aux_done, HALF.done("as3", half - 1))
                parts(mem_k[:, 2 * half:2 * half + 2, :], mk_hi, mk_lo, 2 * half + 1, khalf_ready)
                if half == 0:
                    for t in range(4, 8):
                        main_copied(pool, 0, t)
                else:
                    pool.wait_ge(aux_done, HALF.done("pv1", half - 1))
                parts(mem_v[:, :, half * 256:(half + 1) * 256], mv_hi, mv_lo, 2 * half + 2, vhalf_ready)
            pool.wait_ge(branch_split, 8)
            pool.memset(merged, 0.0).then_inc(merge_done, 1)
            for b in range(TB):
                pool.wait_ge(aux_done, LNT.done("x%d1" % b))
                pool.tensor_scalar(resid[:, b, :], resid[:, b, :], ALPHA, 1.0, ALU.mult, ALU.mult)\
                    .then_inc(resid_ready, 1)

        @block.scalar
        def _(act):
            def hi(s, slot, tiles=None):
                r = slot_raw[0]
                if tiles is not None:
                    act.wait_ge(tile_done, tiles)
                act.wait_ge(slab_landed[r], s * 8 + (16 - 8 * r))
                act.activation(w_hi[:, slot, :], raw[:, r, :], ACT.Copy).then_inc(slab_hi, 1)
                slot_raw[0] = 1 - r

            slot_raw = [0]

            for j in range(4):
                if j == 3:
                    act.wait_ge(front_landed, 16)
                    act.activation(w_hi[:, 0, 0:SLAB // 2], raw[:, 0, 0:SLAB // 2], ACT.Copy).then_inc(front_hi, 1)
                src = aux_of(act, PRO, "t%d" % j).rearrange("p (k m) -> p k m", k=2)
                act.activation(memt_hi[:, 2 * j:2 * j + 2, :], src, ACT.Copy).then_inc(transposed_hi, 1)
            act.wait_ge(slab_landed[0], 16)
            act.activation(w_hi[:, 0, SLAB // 2:SLAB], raw[:, 0, SLAB // 2:SLAB], ACT.Copy).then_inc(slab_hi, 1)
            slot_raw[0] = 1
            hi(1, 1)
            def x_parts(ks):
                for k in ks:
                    act.activation(x_hi[:, k, :], aux_of(act, PRO, "t%d" % (4 + k)), ACT.Copy)\
                        .then_inc(transposed_hi, 1)

            hi(2, 2)
            for s in range(4):
                if s == 2:
                    x_parts(range(0, 4))
                    hi(3, 3)
                    x_parts(range(4, KD))
                    hi(4, 0, 2)
                elif s == 3:
                    hi(5, 1, 4)
                for c in range(2):
                    src = main_of(act, 0, 2 * s + c)[:, 0:M]
                    dst = mem_k[:, 2 * s + c, :] if s < 2 else mem_v[:, c, (s - 2) * 256:(s - 1) * 256]
                    act.activation(dst, src, ACT.Copy).then_inc(main_read[(2 * s + c) % MAIN], 1)
            act.wait_ge(lb_diff, 1)
            act.activation(lbw[:, 1, :], lbw[:, 0, :], ACT.Exp).then_inc(lb_exp, 1)

            with act.Fori(0, 2) as half:
                s0 = half * N_PROJ + S_PROJ
                rnd = proj_round(half)

                def hi_next(r):
                    hi(s0 + (r + 2), (r + 2) % 4, rnd * MAIN + (2 * r - 2))

                hi_next(0)
                act.wait_ge(slab_lo, s0 + 3)
                for h in range(2):
                    act.activation(qm_hi[:, h, :], main_of(act, rnd, h), ACT.Copy).then_inc(qm_rounded, 1)
                hi_next(1)
                for h in range(2):
                    t = main_of(act, rnd, 2 + h)
                    act.activation(lf[:, h, :], t, ACT.Sigmoid)
                    act.activation(kk[:, h, :], t, ACT.Sigmoid, scale=-1.0).then_inc(main_read[2 + h], 1)
                main_copied(act, rnd, 3)
                act.wait_ge(lb_ready, 1)
                for h in range(2):
                    act.activation(lf[:, h, :], lf[:, h, :], ACT.Ln, bias=lbw[:, 4, ds(half * 2 + h, 1)],
                                   scale=lbw[:, 5, ds(half * 2 + h, 1)]).then_inc(logf_ready, 1)
                for b in range(TB):
                    act.wait_ge(negmax_ready, half * TB + (b + 1))
                    for h in range(2):
                        ex = act.activation(probs[:, b, h, :], bank[4 + b][:, h * M:(h + 1) * M], ACT.Exp,
                                            bias=smx[:, 1, b, h:h + 1], scale=SCALE,
                                            accum_out=smx[:, 2, b, h:h + 1])
                    ex.then_inc(aux_read[4 + b], 1)
                hi_next(2)
                for h in range(2):
                    act.activation(qq[:, h, :], main_of(act, rnd, 4 + h), ACT.Sigmoid).then_inc(sig_q, 1)
                act.wait_ge(diffs_ready, half * 2 + 1)
                act.activation(ee, aa, ACT.Exp).then_inc(exps_ready, 1)
                act.activation(aa, aa, ACT.Exp, scale=-1.0).then_inc(exps_ready, 1)
                act.wait_ge(diffs_ready, half * 2 + 2)
                act.activation(bc, bc, ACT.Exp).then_inc(exps_ready, 1)
                act.activation(lf, lf, ACT.Exp).then_inc(exps_ready, 1)
                for b in range(TB):
                    act.activation(y_hi[:, PT_ROW[b], :], aux_of(act, HALF, "pt%d" % b, half), ACT.Copy)\
                        .then_inc(pt_rounded, 1)
                hi_next(3)
                for j in range(2):
                    t = main_of(act, rnd, 6 + j).rearrange("p (b h v) -> p b h v", b=2, h=2)
                    act.activation(v_tok[:, 2 * j:2 * j + 2], t, ACT.Copy).then_inc(main_read[2 + j], 1)
                aux_of(act, HALF, "pv1", half)
                for h in range(2):
                    act.activation(y_hi[:, ds(half * 2 + (8 + h), 1), :], bank[4 + h],
                                   ACT.Copy).then_inc(attn_hi, 1)
                hi_next(4)
                act.wait_ge(operands, half * OPERANDS + 7)
                for h in range(2):
                    act.activation(silu_g[:, h, :], main_of(act, rnd, 8 + h), ACT.Sigmoid).then_inc(sig_g, 1)
                hi_next(5)
                for h in range(2):
                    act.activation(conv_u[:, h, :], main_of(act, rnd, 10 + h), ACT.Copy)\
                        .then_inc(main_read[2 + h], 1)
                    if h == 0:
                        for g in range(2):
                            t = aux_of(act, HALF, "ko%d" % g, half).rearrange("p (b f) -> p b f", b=TB)
                            act.activation(kout_t[:, g], t, ACT.Copy).then_inc(aux_read[6 + g], 1)
                hi_next(6)
                hi_next(7)
                for h in range(2):
                    act.activation(sq_all[:, h, :], aux_of(act, HALF, "out%d" % h, half), ACT.Square)
                    act.activation(sq_hi[:, h, :], bank[4 + h], ACT.Square)\
                        .then_inc(sq_ready, 1)
                for h in range(2):
                    act.activation(o_rstd[:, h, :], aux_of(act, HALF, "ms%d" % h, half), ACT.Ln,
                                   bias=eps[:, 1:2], scale=1.0 / P).then_inc(aux_read[6 + h], 1)
                for h in range(2):
                    aux_copied(act, HALF, "ms%d" % h, half)
                    act.activation(o_rstd[:, h, :], o_rstd[:, h, :], ACT.Exp, scale=-0.5)\
                        .then_inc(rstd_ready, 1)
                for h in range(2):
                    main_copied(act, rnd, 14 + h)
                    act.activation(y_hi[:, ds(half * 2 + h, 1), :], conv_y[:, h, :], ACT.Copy)\
                        .then_inc(conv_hi, 1)
                for h in range(2):
                    act.wait_ge(hgrn_ready, half * 2 + (h + 1))
                    act.activation(y_hi[:, ds(half * 2 + (4 + h), 1), :], o_norm[:, h, :], ACT.Copy)\
                        .then_inc(hgrn_hi, 1)

            def gates(i, last):
                rnd = gate_round(i)
                s0 = i * N_GATE + S_GATE
                free = {0: 0, 1: 2, 2: 4, 3: 8, 4: 10, 5: 12}

                def hi_gate(r):
                    hi(s0 + (r + 2), (r + 2) % 3, rnd * MAIN + free[r])

                for h in range(2):
                    for j in range(2):
                        hi_gate(3 * h + j)
                        if j == 0:
                            act.wait_ge(merge_done, i * 8 + (4 * h + 1))
                        for t in (2 * j, 2 * j + 1):
                            act.activation(tiles4[:, t, :], main_of(act, rnd, 8 * h + t), ACT.Sigmoid,
                                           bias=par[:, ds(i * 8 + (4 * h + t), 1)]).then_inc(main_read[t], 1)
                    if last and h == 1:
                        merged_parts(0)
                    hi_gate(3 * h + 2)

            def merged_parts(h):
                for k in range(4 * h, 4 * h + 4):
                    act.wait_ge(merge_done, 1 + 2 * KD + k + 1)
                    act.activation(y_hi[:, k, :], merged[:, k, :], ACT.Copy).then_inc(merged_hi, 1)

            with act.Fori(0, 2) as i:
                gates(i, False)
            gates(2, True)
            hi(S_OUT + 2, 3)
            merged_parts(1)
            hi(S_OUT + 3, 2, OUT_ROUND * MAIN)

            def norm(n):
                act.wait_ge(var_ready, n + 1)
                act.activation(lnw[:, 0:1], mv[:, 1:2], ACT.Sqrt, bias=eps[:, 0:1]).then_inc(std_ready, 1)

            def x1_parts(b):
                for j in range(2):
                    t = aux_of(act, LNT, "x%d%d" % (b, j)).rearrange("p (k t) -> p k t", k=4)
                    act.activation(x_hi[:, 4 * j:4 * j + 4, b * P:(b + 1) * P], t, ACT.Copy).then_inc(x1_hi, 1)

            norm(0)
            norm(1)
            x1_parts(0)
            norm(2)
            x1_parts(1)
            hi(S_MLP, 0, OUT_ROUND * MAIN + 7)
            hi(S_MLP + 1, 1, OUT_ROUND * MAIN + 7)
            norm(3)
            x1_parts(2)
            x1_parts(3)

            def mlp(g, last):
                rnd = mlp_round(g)
                s0 = g * N_MLP + S_MLP
                m0 = rnd * MAIN

                def hidden(u):
                    act.activation(tiles4[:, u % 2, :], main_of(act, rnd, u), ACT.Relu)\
                        .then_inc(main_read[u % MAIN], 1)
                    main_copied(act, rnd, u)
                    act.activation(y_hi[:, u, :], tiles4[:, u % 2, :], ACT.Square).then_inc(h_hi, 1)

                for j in range(4):
                    if j < 2:
                        hi(s0 + (j + 2), j + 2, m0)
                    elif j == 2:
                        hi(s0 + 4, 0, m0 + 2)
                    else:
                        hi(s0 + 5, 1, m0 + 4)
                        hi(s0 + 6, 2, m0 + 6)
                    for u in (2 * j, 2 * j + 1):
                        if u >= 2:
                            act.wait_ge(h_split, g * 8 + (u - 1))
                        elif u == 0:
                            act.wait_ge(slab_lo, s0 + 3)
                        hidden(u)
                hi(s0 + 7, 3, m0 + 8)
                if not last:
                    hi(s0 + 8, 0, m0 + 15)
                    hi(s0 + 9, 1, m0 + 15)
                else:
                    for b in range(TB):
                        norm(TB + b)

            with act.Fori(0, G_MLP - 1) as g:
                mlp(g, False)
            mlp(G_MLP - 1, True)

        @block.vector
        def _(dve):
            raw_slot = [0]

            def lo(s, slot):
                r = raw_slot[0]
                dve.wait_ge(slab_hi, s + 1)
                dve.tensor_tensor(w_lo[:, slot, :], raw[:, r, :], w_hi[:, slot, :].bitcast(F32), ALU.subtract)\
                    .then_inc(slab_lo, 1)
                raw_slot[0] = 1 - r

            def low_of(dst, src, high):
                return dve.tensor_tensor(dst, src, high.bitcast(F32), ALU.subtract)

            for j in range(4):
                if j == 3:
                    dve.wait_ge(front_hi, 1)
                    part = slice(0, SLAB // 2)
                    low_of(w_lo[:, 0, part], raw[:, 0, part], w_hi[:, 0, part]).then_inc(front_lo, 1)
                dve.wait_ge(transposed_hi, j + 1)
                src = bank[PRO.bank["t%d" % j]].rearrange("p (k m) -> p k m", k=2)
                low_of(memt_lo[:, 2 * j:2 * j + 2, :], src, memt_hi[:, 2 * j:2 * j + 2, :])\
                    .then_inc(aux_read[PRO.bank["t%d" % j]], 1)
            dve.wait_ge(slab_hi, 1)
            part = slice(SLAB // 2, SLAB)
            low_of(w_lo[:, 0, part], raw[:, 0, part], w_hi[:, 0, part]).then_inc(slab_lo, 1)
            raw_slot[0] = 1
            lo(1, 1)
            def x_parts(ks):
                for k in ks:
                    n = "t%d" % (4 + k)
                    dve.wait_ge(transposed_hi, 4 + k + 1)
                    low_of(x_lo[:, k, :], bank[PRO.bank[n]], x_hi[:, k, :]).then_inc(aux_read[PRO.bank[n]], 1)

            lo(2, 2)
            x_parts(range(0, 4))
            lo(3, 3)
            x_parts(range(4, KD))
            lo(4, 0)
            lo(5, 1)
            dve.tensor_copy(par[:], aux_of(dve, PRO, "t12")[:, 0:41]).then_inc(aux_read[4], 1)
            aux_copied(dve, PRO, "t12")
            lb_raw = par[:, LB:LB + HEADS]
            dve.tensor_tensor(lbw[:, 0, :], lb_raw, lb_raw, ALU.subtract).then_inc(lb_diff, 1)
            dve.wait_ge(lb_exp, 1)
            dve.reciprocal(lbw[:, 2, :], lbw[:, 1, :]).then_inc(dve_chain, 1)
            dve.wait_ge(dve_chain, 1)
            dve.tensor_tensor(lbw[:, 3, :], lbw[:, 1, :], lbw[:, 2, :], ALU.mult).then_inc(dve_chain, 1)
            dve.wait_ge(dve_chain, 2)
            dve.tensor_tensor(lbw[:, 4, :], lbw[:, 3, :], lbw[:, 3, :], ALU.subtract).then_inc(dve_chain, 1)
            dve.wait_ge(dve_chain, 3)
            dve.tensor_scalar(lbw[:, 5, :], lbw[:, 4, :], -1.0, 1.0, ALU.mult, ALU.add).then_inc(lb_ready, 1)
            dve.wait_ge(consts_ready, 1)
            dve.wait_ge(lb_ready, 1)

            CHAIN_HALF = 15
            STATES_HALF = 4

            with dve.Fori(0, 2) as half:
                s0 = half * N_PROJ + S_PROJ
                rnd = proj_round(half)
                chain = [0]

                def link(ins):
                    ins.then_inc(dve_chain, 1)
                    chain[0] += 1
                    return chain[0]

                def linked(n):
                    dve.wait_ge(dve_chain, half * CHAIN_HALF + (3 + n))

                def omlb(h):
                    return lbw[:, 5, ds(half * 2 + h, 1)]

                lo(s0 + 2, 2)
                for h in range(2):
                    dve.wait_ge(qm_rounded, half * 2 + (h + 1))
                    low_of(qm_lo[:, h, :], bank[h], qm_hi[:, h, :]).then_inc(main_read[h], 1)
                lo(s0 + 3, 3)
                for b in range(TB):
                    t = aux_of(dve, HALF, "as%d" % b, half).rearrange("p (h m) -> p h m", h=2)
                    n = link(dve.tensor_reduce(smx[:, 0, b, :], t, AX_X, ALU.max))
                    linked(n)
                    dve.tensor_scalar(smx[:, 1, b, :], smx[:, 0, b, :], -SCALE, None, ALU.mult)\
                        .then_inc(negmax_ready, 1)
                for h in range(2):
                    dve.wait_ge(logf_ready, half * 2 + (h + 1))
                    n = link(dve.tensor_tensor_scan(bc[:, h, :], scan_keep[:], lf[:, h, :], 0.0,
                                                    ALU.mult, ALU.add))
                linked(n)
                b3 = chunks(bc)
                mid = b3[:, :, C // 2 - 1:C // 2].to_broadcast((P, 2 * NCH, C))
                end = b3[:, :, C - 1:C].to_broadcast((P, 2 * NCH, C))
                dve.tensor_tensor(chunks(aa), b3, mid, ALU.subtract).then_inc(diffs_ready, 1)
                dve.tensor_tensor(chunks(lf), end, b3, ALU.subtract).then_inc(diffs_ready, 1)
                for b in range(TB):
                    aux_copied(dve, HALF, "as%d" % b, half)
                n = link(dve.reciprocal(smx[:, 3], smx[:, 2]))
                linked(n)
                for b in range(TB):
                    for h in range(2):
                        pr = dve.tensor_scalar(probs[:, b, h, :], probs[:, b, h, :], smx[:, 3, b, h:h + 1],
                                               None, ALU.mult)
                    pr.then_inc(probs_ready, 1)
                lo(s0 + 4, 0)
                for h in range(2):
                    dve.wait_ge(sig_q, half * 2 + (h + 1))
                    dve.tensor_tensor(qq[:, h, :], qq[:, h, :], bank[h], ALU.mult).then_inc(main_read[h], 1)
                for b in range(TB):
                    dve.wait_ge(pt_rounded, half * TB + (b + 1))
                    low_of(y_lo[:, PT_ROW[b], :], bank[4 + b], y_hi[:, PT_ROW[b], :])\
                        .then_inc(aux_read[4 + b], 1)
                lo(s0 + 5, 1)
                dve.wait_ge(exps_ready, half * 4 + 4)
                for h in range(2):
                    dve.scalar_tensor_tensor(lf[:, h, :], kk[:, h, :], omlb(h), lf[:, h, :], ALU.mult, ALU.mult)\
                        .then_inc(operands, 1)
                for h in range(2):
                    dve.scalar_tensor_tensor(aa[:, h, :], kk[:, h, :], omlb(h), aa[:, h, :], ALU.mult, ALU.mult)\
                        .then_inc(operands, 1)
                main_copied(dve, rnd, 4)
                main_copied(dve, rnd, 5)
                dve.tensor_tensor(ee, ee, qq, ALU.mult).then_inc(operands, 1)
                dve.tensor_tensor(qq, qq, bc, ALU.mult).then_inc(operands, 1)
                dve.tensor_copy(decay[:].rearrange("p n q -> p (n q)").unsqueeze(2), b3[:, :, C - 1:C])\
                    .then_inc(operands, 1)
                for h in range(2):
                    dve.wait_ge(attn_hi, half * 2 + (h + 1))
                    r = ds(half * 2 + (8 + h), 1)
                    low_of(y_lo[:, r, :], bank[4 + h].unsqueeze(1), y_hi[:, r, :]).then_inc(aux_read[4 + h], 1)
                dve.wait_ge(operands, half * OPERANDS + 7)
                k_out = lf.rearrange("p h (b c) -> p (h b) c", b=TB)

                def over(q, width):
                    return decay[:, :, q:q + 1].to_broadcast((P, 2 * TB, width))

                dve.tensor_tensor(k_two[:, :, 0:C], k_out[:, :, 0:C], over(1, C), ALU.mult)
                dve.tensor_copy(k_two[:, :, C:2 * C], k_out[:, :, C:2 * C])
                dve.tensor_copy(k_three[:, :, 2 * C:3 * C], k_out[:, :, 2 * C:3 * C])
                n = link(dve.tensor_copy(decays[:, :, 1:2], decay[:, :, 0:1]))
                linked(n)
                dve.tensor_tensor(k_three[:, :, 0:2 * C], k_two, over(2, 2 * C), ALU.mult).then_inc(operands, 1)
                for q in range(1, QD):
                    n = link(dve.tensor_tensor(decays[:, :, q + 1:q + 2], decays[:, :, q:q + 1],
                                               decay[:, :, q:q + 1], ALU.mult))
                    linked(n)
                lo(s0 + 6, 2)
                for h in range(2):
                    aux_of(dve, HALF, "sc%d" % h, half)
                    dve.wait_ge(sig_g, half * 2 + (h + 1))
                    dve.tensor_tensor(silu_g[:, h, :], silu_g[:, h, :], bank[h], ALU.mult)\
                        .then_inc(main_read[h], 1)
                seen = causal[:].unsqueeze(1).to_broadcast((P, TB, P))
                for h in range(2):
                    t = bank[4 + h].rearrange("p (b t) -> p b t", b=TB)
                    dve.copy_predicated(sc_causal[:, h], seen, t).then_inc(aux_read[4 + h], 1)
                dve.tensor_tensor(k_out[:, :, 0:3 * C], k_three, over(3, 3 * C), ALU.mult).then_inc(operands, 1)
                dve.tensor_tensor(q_block.rearrange("p h (b q c) -> p (h b) q c", b=TB, q=QD),
                                  qq.rearrange("p h (b q c) -> p (h b) q c", b=TB, q=QD),
                                  decays[:, :, 0:QD].unsqueeze(3).to_broadcast((P, 2 * TB, QD, C)), ALU.mult)\
                    .then_inc(operands, 1)
                lo(s0 + 7, 3)
                aux_of(dve, HALF, "kv1", half)
                for b in range(TB - 1):
                    for h in range(2):
                        kv = bank[6 + h][:, b * P:(b + 1) * P]
                        if b == 0:
                            st = dve.tensor_copy(states[:, h, 0, :], kv)
                        else:
                            n = h * TB + b
                            st = dve.scalar_tensor_tensor(states[:, h, b, :], states[:, h, b - 1, :],
                                                          decays[:, n, QD:QD + 1], kv, ALU.mult, ALU.add)
                        st.then_inc(state_step if b < TB - 2 else aux_read[6 + h], 1)
                    if b < TB - 2:
                        dve.wait_ge(state_step, half * STATES_HALF + 2 * (b + 1))
                lo(s0 + 8, 0)
                for h in range(2):
                    main_copied(dve, rnd, 10 + h)
                    dve.tensor_tensor(conv_u[:, h, :], conv_u[:, h, :], main_of(dve, rnd, 12 + h), ALU.mult)\
                        .then_inc(main_read[h], 1)
                    if h == 0:
                        for g in range(2):
                            dve.wait_ge(sq_ready, half * 2 + (g + 1))
                            low_of(sq_lo[:, g, :], sq_all[:, g, :], sq_hi[:, g, :]).then_inc(sq_split, 1)
                for h in range(2):
                    main_copied(dve, rnd, 12 + h)

                    def tap(n, h=h):
                        return par[:, ds(half * 2 + (CONV_W + 4 * n + h), 1)]

                    n = link(dve.tensor_scalar(conv_y[:, h, :], conv_u[:, h, :], tap(2), None, ALU.mult))
                    for back in (1, 2):
                        linked(n)
                        st = dve.scalar_tensor_tensor(conv_y[:, h, back:T], conv_u[:, h, 0:T - back],
                                                      tap(2 - back), conv_y[:, h, back:T], ALU.mult, ALU.add)
                        if back == 1:
                            n = link(st)
                        else:
                            st.then_inc(conv_tapped, 1)
                lo(s0 + 9, 1)
                for h in range(2):
                    dve.wait_ge(conv_tapped, half * 2 + (h + 1))
                    t = main_of(dve, rnd, 14 + h)
                    dve.tensor_tensor(conv_y[:, h, :], conv_y[:, h, :], t, ALU.mult).then_inc(main_read[2 + h], 1)
                for h in range(2):
                    r = ds(half * 2 + h, 1)
                    dve.wait_ge(conv_hi, half * 2 + (h + 1))
                    low_of(y_lo[:, r, :], conv_y[:, h:h + 1, :], y_hi[:, r, :]).then_inc(branch_split, 1)
                for h in range(2):
                    dve.wait_ge(rstd_ready, half * 2 + (h + 1))
                    dve.scalar_tensor_tensor(o_norm[:, h, :], bank[4 + h], par[:, NORM_W:NORM_W + 1],
                                             o_rstd[:, h, :], ALU.mult, ALU.mult).then_inc(aux_read[4 + h], 1)
                for h in range(2):
                    aux_copied(dve, HALF, "out%d" % h, half)
                    main_copied(dve, rnd, 8 + h)
                    dve.tensor_tensor(o_norm[:, h, :], o_norm[:, h, :], silu_g[:, h, :], ALU.mult)\
                        .then_inc(hgrn_ready, 1)
                for h in range(2):
                    r = ds(half * 2 + (4 + h), 1)
                    dve.wait_ge(hgrn_hi, half * 2 + (h + 1))
                    low_of(y_lo[:, r, :], o_norm[:, h:h + 1, :], y_hi[:, r, :]).then_inc(branch_split, 1)
                assert chain[0] == CHAIN_HALF, chain

            def gates(i, last):
                rnd = gate_round(i)
                s0 = i * N_GATE + S_GATE
                for h in range(2):
                    for j in range(3):
                        r = 3 * h + j + 2
                        lo(s0 + r, r % 3)
                        if last and h == 1 and j == 1:
                            merged_parts(0)
                    dve.wait_ge(merge_done, i * 8 + (4 * h + 1))
                    for t in range(4):
                        main_copied(dve, rnd, 8 * h + t)
                        src = main_of(dve, rnd, 8 * h + 4 + t)
                        dve.tensor_tensor(tiles4[:, t, :], tiles4[:, t, :], src, ALU.mult)\
                            .then_inc(main_read[t], 1)
                        main_copied(dve, rnd, 8 * h + 4 + t)
                        k = 4 * h + t
                        dve.tensor_tensor(merged[:, k, :], merged[:, k, :], tiles4[:, t, :], ALU.add)\
                            .then_inc(merge_done, 1)

            def merged_parts(h):
                for k in range(4 * h, 4 * h + 4):
                    dve.wait_ge(merged_hi, k + 1)
                    low_of(y_lo[:, k, :], merged[:, k, :], y_hi[:, k, :]).then_inc(merged_split, 1)

            with dve.Fori(0, 2) as i:
                gates(i, False)
            gates(2, True)
            merged_parts(1)
            lo(S_OUT + 2, 3)
            lo(S_OUT + 3, 2)

            ln_chain = [0]

            def ln_link(ins):
                ins.then_inc(ln_step, 1)
                ln_chain[0] += 1
                dve.wait_ge(ln_step, ln_chain[0])

            def half_of(b, e):
                return resid[:, b, e * WID:(e + 1) * WID]

            def norm(n, done):
                b = n % TB
                p = 2 * (n // TB)
                dve.bn_aggr(mv[:], stats[:].rearrange("p e s -> p (e s)")).then_inc(var_ready, 1)
                dve.wait_ge(var_ready, n + 1)
                for e in range(2):
                    dve.scalar_tensor_tensor(half_of(b, e), half_of(b, e), mv[:, 0:1],
                                             ln_par[:, p, e * WID:(e + 1) * WID], ALU.subtract, ALU.mult)
                dve.wait_ge(std_ready, n + 1)
                ln_link(dve.reciprocal(lnw[:, 1:2], lnw[:, 0:1]))
                for e in range(2):
                    dve.scalar_tensor_tensor(half_of(b, e), half_of(b, e), lnw[:, 1:2],
                                             ln_par[:, p + 1, e * WID:(e + 1) * WID], ALU.mult, ALU.add)\
                        .then_inc(done, 1)

            def stats_of(rnd, t, b, e):
                main_copied(dve, rnd, t)
                st = dve.bn_stats(stats[:, e, :], half_of(b, e))
                if e == 1:
                    ln_link(st)

            def x1_parts(b):
                for j in range(2):
                    dve.wait_ge(x1_hi, 2 * b + j + 1)
                    n = "x%d%d" % (b, j)
                    part = (slice(None), slice(4 * j, 4 * j + 4), slice(b * P, (b + 1) * P))
                    low_of(x_lo[part], bank[LNT.bank[n]].rearrange("p (k t) -> p k t", k=4), x_hi[part])\
                        .then_inc(aux_read[LNT.bank[n]], 1)

            dve.wait_ge(x_again, 16)
            dve.wait_ge(ln_landed, 64)

            def mixed(b, e):
                w = 2 * b + e
                z = resid[:, b, e * WID:(e + 1) * WID]
                dve.scalar_tensor_tensor(z, z, ALPHA, main_of(dve, OUT_ROUND, w), ALU.mult, ALU.add)\
                    .then_inc(main_read[w % MAIN], 1)

            for b in range(TB):
                mixed(b, 0)
                stats_of(OUT_ROUND, 2 * b, b, 0)
                if b == TB - 1:
                    lo(S_MLP, 0)
                    lo(S_MLP + 1, 1)
                mixed(b, 1)
                stats_of(OUT_ROUND, 2 * b + 1, b, 1)
                norm(b, x1_ready)
                if b:
                    x1_parts(b - 1)
            x1_parts(TB - 1)

            def mlp(g, last):
                rnd = mlp_round(g)
                s0 = g * N_MLP + S_MLP
                for j in range(4):
                    for s in ((2,), (3,), (4,), (5, 6))[j]:
                        lo(s0 + s, s % 4)
                    for u in (2 * j, 2 * j + 1):
                        main_copied(dve, rnd, u)
                        r, h = tiles4[:, u % 2, :], tiles4[:, 2 + u % 2, :]
                        dve.tensor_tensor(h, r, r, ALU.mult).then_inc(h_made, 1)
                        dve.wait_ge(h_made, g * 8 + (u + 1))
                        dve.wait_ge(h_hi, g * 8 + (u + 1))
                        low_of(y_lo[:, u, :], h, y_hi[:, u, :]).then_inc(h_split, 1)
                lo(s0 + 7, 3)
                for w in range(2 * TB):
                    b, e = divmod(w, 2)
                    z = resid[:, b, e * WID:(e + 1) * WID]
                    dve.wait_ge(resid_ready, b + 1)
                    dve.wait_ge(main_read[w % MAIN], rnd + ((8 + w) // MAIN))
                    dve.tensor_tensor(z, z, main_of(dve, rnd, 8 + w), ALU.add).then_inc(main_read[w % MAIN], 1)
                    if not last and w == 2 * TB - 2:
                        lo(s0 + 8, 0)
                        lo(s0 + 9, 1)
                    if last:
                        stats_of(rnd, 8 + w, b, e)
                        if e == 1:
                            norm(TB + b, y_ready)

            with dve.Fori(0, G_MLP - 1) as g:
                mlp(g, False)
            mlp(G_MLP - 1, True)

        @block.tensor
        def _(pe):
            def begin(rnd, t):
                r = rnd + t // MAIN
                if not isinstance(r, int) or r > 0:
                    pe.wait_ge(main_read[t % MAIN], r)
                return bank[t % MAIN]

            def begin_aux(phase, name, it=0):
                n = phase.earlier(name, it)
                if not isinstance(n, int) or n > 0:
                    pe.wait_ge(aux_read[phase.bank[name]], n)
                return bank[phase.bank[name]]

            def slab(s):
                pe.wait_ge(slab_lo, s + 1)

            def three(dst, a, b, first, last):
                pe.matmul(dst, a[0], b[0], start=first, stop=False)
                pe.matmul(dst, a[0], b[1], start=False, stop=False)
                return pe.matmul(dst, a[1], b[0], start=False, stop=last)

            def w_part(slot, at, n):
                return w_hi[:, slot, at:at + n], w_lo[:, slot, at:at + n]

            def both(hi_, lo_, *at):
                return hi_[at], lo_[at]

            ALL = slice(None)

            pe.wait_ge(ident_ready, 1)
            for j in range(4):
                if j % 2 == 0:
                    pe.wait_ge(mem_landed[j // 2], 16)
                t = begin_aux(PRO, "t%d" % j)
                for k in range(2):
                    for b in range(2):
                        c = (2 * j + k) * P
                        tr = pe.transpose(t[:, (2 * k + b) * P:(2 * k + b + 1) * P], mem_tok[:, b, c:c + P],
                                          ident[:])
                tr.then_inc(aux_done, 1)

            def x_transposed(ks):
                for k in ks:
                    t = begin_aux(PRO, "t%d" % (4 + k))
                    for b in range(TB):
                        tr = pe.transpose(t[:, b * P:(b + 1) * P], x_tok[:, b, k * P:(k + 1) * P], ident[:])
                    tr.then_inc(aux_done, 1)

            for s in range(4):
                if s == 2:
                    pe.wait_ge(x_landed, 16)
                    x_transposed(range(0, 4))
                if s:
                    slab(s)
                for c in range(2):
                    if s == 2 and c == 1:
                        x_transposed(range(4, KD))
                    t = begin(0, 2 * s + c)[:, 0:M]
                    for k in range(KD):
                        if s == 0 and c == 0:
                            if k == 0:
                                pe.wait_ge(front_lo, 1)
                            if k == KD // 2:
                                slab(0)
                            if k % 2 == 0:
                                aux_copied(pe, PRO, "t%d" % (k // 2))
                        if s < 2:
                            mm = three(t, w_part(s, k * 256 + c * P, P), both(memt_hi, memt_lo, ALL, k),
                                       k == 0, k == KD - 1)
                        else:
                            mm = three(t, both(memt_hi, memt_lo, ALL, k, slice(c * P, (c + 1) * P)),
                                       w_part(s, k * 256, 256), k == 0, k == KD - 1)
                    mm.then_inc(tile_done, 1)
            pe.wait_ge(small_landed, 64)
            pe.transpose(begin_aux(PRO, "t12")[:, 0:41], par_rows, ident[0:41, 0:41]).then_inc(aux_done, 1)

            def feature_part(dst, tokens, slot, c):
                for k in range(KD):
                    mm = three(dst[:, tokens], w_part(slot, k * 256 + c * P, P), both(x_hi, x_lo, ALL, k, tokens),
                               k == 0, k == KD - 1)
                return mm

            def feature_tile(rnd, t, slot, c):
                feature_part(begin(rnd, t), slice(0, T), slot, c).then_inc(tile_done, 1)

            for k in range(4, 12):
                aux_copied(pe, PRO, "t%d" % k)

            with pe.Fori(0, 2) as half:
                rnd = proj_round(half)
                s0 = half * N_PROJ + S_PROJ

                def blk(b):
                    return slice(b * P, (b + 1) * P)

                def slab_tiles(j):
                    slab(s0 + j)
                    for c in range(2):
                        feature_tile(rnd, 2 * j + c, j % 4, c)

                slab_tiles(0)
                slab_tiles(1)
                for h in range(2):
                    main_copied(pe, rnd, h)
                pe.wait_ge(khalf_ready, half + 1)
                for b in range(TB):
                    t = begin_aux(HALF, "as%d" % b, half)
                    for h in range(2):
                        mm = three(t[:, h * M:(h + 1) * M], both(qm_hi, qm_lo, ALL, h, blk(b)),
                                   both(mk_hi, mk_lo, ALL, h), True, True)
                    mm.then_inc(aux_done, 1)
                slab_tiles(2)
                for b in range(TB):
                    pe.wait_ge(probs_ready, half * TB + (b + 1))
                    t = begin_aux(HALF, "pt%d" % b, half)
                    for h in range(2):
                        for m in range(2):
                            tr = pe.transpose(t[:, blk(2 * h + m)], probs[:, b, h, blk(m)], ident[:])
                    tr.then_inc(aux_done, 1)
                slab(s0 + 3)
                for j in range(2):
                    dst = begin(rnd, 6 + j)
                    for b in range(2):
                        for k in range(KD):
                            mm = three(dst[:, b * 256:(b + 1) * 256],
                                       both(x_hi, x_lo, ALL, k, blk(2 * j + b)), w_part(3, k * 256, 256),
                                       k == 0, k == KD - 1)
                    mm.then_inc(tile_done, 1)
                pe.wait_ge(vhalf_ready, half + 1)
                for b in range(TB):
                    aux_copied(pe, HALF, "pt%d" % b, half)
                for h in range(2):
                    t = begin_aux(HALF, "pv%d" % h, half)
                    for c in range(2):
                        blocks = slice(PT_ROW[2 * c], PT_ROW[2 * c] + 2)
                        for m in range(2):
                            mm = three(t[:, c * 2 * P:(c + 1) * 2 * P].rearrange("p (b t) -> p b t", b=2),
                                       both(mv_hi, mv_lo, ALL, m, blk(h)),
                                       both(y_hi, y_lo, ALL, blocks, blk(2 * h + m)), m == 0, m == 1)
                    mm.then_inc(aux_done, 1)
                slab_tiles(4)
                pe.wait_ge(operands, half * OPERANDS + 8)
                for h in range(2):
                    t = begin_aux(HALF, "sc%d" % h, half)
                    for b in range(TB):
                        pe.matmul(t[:, blk(b)], aa[:, h, blk(b)], ee[:, h, blk(b)], start=True, stop=True)
                        for q in range(1, QD):
                            n = h * TB + b
                            now = slice(b * P + q * C, b * P + (q + 1) * C)
                            keys = (lf[:, h, b * P:b * P + C], k_two[:, n, :], k_three[:, n, :])[q - 1]
                            mm = pe.matmul(t[0:q * C, now], keys, qq[:, h, now], start=True, stop=True)
                    mm.then_inc(aux_done, 1)
                slab(s0 + 5)
                feature_tile(rnd, 10, 1, 0)
                pe.wait_ge(operands, half * OPERANDS + 9)
                for h in range(2):
                    t = begin_aux(HALF, "ko%d" % h, half)
                    for b in range(TB):
                        tr = pe.transpose(t[:, blk(b)], lf[:, h, blk(b)], ident[:])
                    tr.then_inc(aux_done, 1)
                feature_tile(rnd, 11, 1, 1)
                for h in range(2):
                    main_copied(pe, rnd, 6 + h)
                for h in range(2):
                    t = begin_aux(HALF, "kv%d" % h, half)
                    for b in range(TB - 1):
                        mm = pe.matmul(t[:, blk(b)], kout_t[:, h, b, :], v_tok[:, b, h, :], start=True, stop=True)
                    mm.then_inc(aux_done, 1)
                slab(s0 + 6)
                feature_tile(rnd, 12, 2, 0)
                pe.wait_ge(operands, half * OPERANDS + 10)
                for h in range(2):
                    t = begin_aux(HALF, "out%d" % h, half)
                    aux_copied(pe, HALF, "kv%d" % h, half)
                    for b in range(TB):
                        mm = pe.matmul(t[:, blk(b)], v_tok[:, b, h, :], sc_causal[:, h, b, :], start=b == 0,
                                       stop=False)
                        if b:
                            mm = pe.matmul(t[:, blk(b)], states[:, h, b - 1, :], q_block[:, h, blk(b)],
                                           start=False, stop=b == TB - 1)
                    mm.then_inc(aux_done, 1)
                feature_tile(rnd, 13, 2, 1)
                slab(s0 + 7)
                feature_tile(rnd, 14, 3, 0)
                pe.wait_ge(consts_ready, 1)
                for h in range(2):
                    pe.wait_ge(sq_split, half * 2 + (h + 1))
                    t = begin_aux(HALF, "ms%d" % h, half)
                    pe.matmul(t, ones[:], sq_hi[:, h, :], start=True, stop=False)
                    pe.matmul(t, ones[:], sq_lo[:, h, :], start=False, stop=True).then_inc(aux_done, 1)
                feature_tile(rnd, 15, 3, 1)

            with pe.Fori(0, 3) as i:
                rnd = gate_round(i)
                s0 = i * N_GATE + S_GATE
                for h in range(2):
                    for j in range(2):
                        r = 3 * h + j
                        slab(s0 + r)
                        for c in range(2):
                            feature_tile(rnd, 8 * h + 2 * j + c, r % 3, c)
                    slab(s0 + (3 * h + 2))
                    pe.wait_ge(branch_split, 8)
                    for c in range(4):
                        dst = begin(rnd, 8 * h + 4 + c)
                        for k in range(HEADS):
                            mm = three(dst, w_part(2, k * WID + c * P, P),
                                       both(y_hi, y_lo, ALL, ds(i * HEADS + k, 1)), k == 0, k == HEADS - 1)
                        mm.then_inc(tile_done, 1)

            def token_chunk(dst, b, e, k, slots):
                return three(dst, both(y_hi, y_lo, ALL, k, slice(b * P, (b + 1) * P)),
                             w_part(slots[e][k // 4], (k % 4) * WID, WID), k == 0, k == KD - 1)

            def token_tiles(rnd, t0, slots, first):
                for b in range(TB):
                    for e in range(2):
                        dst = begin(rnd, t0 + 2 * b + e)
                        for k in range(KD):
                            if b == 0:
                                first(e, k)
                            mm = token_chunk(dst, b, e, k, slots)
                        mm.then_inc(tile_done, 1)

            def x1_transposed(b):
                pe.wait_ge(x1_ready, 2 * (b + 1))
                for j in range(2):
                    t = begin_aux(LNT, "x%d%d" % (b, j))
                    for k in range(4):
                        c = (4 * j + k) * P
                        tr = pe.transpose(t[:, k * P:(k + 1) * P], resid[:, b, c:c + P], ident[:])
                    tr.then_inc(aux_done, 1)

            out_slots = ((0, 1), (3, 2))
            slab(S_OUT)
            for b in range(2):
                dst = begin(OUT_ROUND, 2 * b)
                for k in range(4):
                    if b == 0:
                        pe.wait_ge(merged_split, k + 1)
                    token_chunk(dst, b, 0, k, out_slots)
            for b in range(TB):
                for e in range(2):
                    begun = b < 2 and e == 0
                    dst = bank[2 * b] if begun else begin(OUT_ROUND, 2 * b + e)
                    for k in range(4 if begun else 0, KD):
                        if b == 0 and k % 4 == 0:
                            slab(S_OUT + 2 * e + k // 4)
                        if b == 0 and begun:
                            pe.wait_ge(merged_split, k + 1)
                        mm = token_chunk(dst, b, e, k, out_slots)
                    mm.then_inc(tile_done, 1)
                if b:
                    x1_transposed(b - 1)

            for b in range(2):
                for j in range(2):
                    aux_copied(pe, LNT, "x%d%d" % (b, j))
            for u in range(4):
                if u % 2 == 0:
                    slab(S_MLP + u // 2)
                if u == 3:
                    x1_transposed(TB - 1)
                feature_part(begin(mlp_round(0), u), slice(0, T // 2), u // 2, u % 2)
            for b in range(2, TB):
                for j in range(2):
                    aux_copied(pe, LNT, "x%d%d" % (b, j))
            for u in range(4):
                feature_part(bank[u], slice(T // 2, T), u // 2, u % 2).then_inc(tile_done, 1)

            def mlp(g, begun=0):
                rnd = mlp_round(g)
                s0 = g * N_MLP + S_MLP
                for j in range(begun, 4):
                    slab(s0 + j)
                    for c in range(2):
                        feature_tile(rnd, 2 * j + c, j, c)

                def first(e, k):
                    if k % 4 == 0:
                        slab(s0 + (4 + 2 * e + k // 4))
                    if e == 0:
                        pe.wait_ge(h_split, g * 8 + (k + 1))

                token_tiles(rnd, 8, ((0, 1), (2, 3)), first)

            mlp(0, 2)
            with pe.Fori(1, G_MLP) as g:
                mlp(g)


_INS = ["x", "mem", "lower_bounds", "w_in", "conv_w", "hg_norm_w", "w_mem_k", "w_mem_v", "w_branch", "b_gate",
        "w_o", "ln1_g", "ln1_b", "w_up", "w_down", "ln2_g", "ln2_b"]


def kernel(**inputs):
    import numpy as _np
    import concourse.bacc as _bacc
    from concourse import mybir as _mybir
    from concourse.bass_utils import run_bass_kernel_spmd as _run

    nc = _bacc.Bacc("TRN2", target_bir_lowering=False, num_devices=1, dynamic_dma_scratch_size=1024)
    arrays, args = {}, []
    for name in _INS:
        a = _np.ascontiguousarray(inputs[name])
        arrays[f"in_{name}_dram"] = a
        args.append(nc.dram_tensor(f"in_{name}_dram", a.shape, _mybir.dt.from_np(a.dtype), kind="ExternalInput").ap())
    args.append(nc.dram_tensor("out_dram", inputs["x"].shape, _mybir.dt.float32, kind="ExternalOutput").ap())
    build(nc, *args)
    r = _run(nc, [arrays], core_ids=[0])
    return r.results[0]["out_dram"]
```
